# Optimizing a Trainium2 kernel written in Bass

```python
import math
import jax, jax.numpy as jnp
from jax import lax
import numpy as np

D_MODEL = 1024
BATCH = 1
SEQ = 256
DEPTH = 2

RMS_EPS = 1e-6
MASK_VALUE = -1e30
LB_FLOOR = 1e-20
ATT_DK = 64
ATT_HEADS = D_MODEL // (2 * ATT_DK)
ATT_DV = 2 * ATT_DK
ATT_QK_WIDTH = ATT_HEADS * 2 * ATT_DK
ATT_V_WIDTH = ATT_HEADS * ATT_DV
ATT_BLOCK = 128
POOL_WINDOWS = (2, 4, 8, 16)
POOL_GROUPS = 4
POOL_WIDTH = D_MODEL
POOL_GW = POOL_WIDTH // POOL_GROUPS
HGRN_DK = 128
HGRN_DV = 128
HGRN_HEADS = D_MODEL // HGRN_DV
HGRN_K_WIDTH = HGRN_HEADS * HGRN_DK
HGRN_V_WIDTH = HGRN_HEADS * HGRN_DV
HGRN_CHUNK = 64
N_BRANCHES = 3
IN_SIZES = (ATT_QK_WIDTH, ATT_QK_WIDTH, ATT_V_WIDTH, POOL_WIDTH,
            HGRN_K_WIDTH, HGRN_K_WIDTH, HGRN_V_WIDTH, HGRN_V_WIDTH, N_BRANCHES * D_MODEL)
IN_COLS = sum(IN_SIZES)
PEER_HEADS = 8
PEER_DQ = 256
PEER_DHALF = PEER_DQ // 2
PEER_NKEYS = 128
PEER_NEXPERTS = PEER_NKEYS * PEER_NKEYS
PEER_TOPK = 16
PEER_TOKEN_BLOCK = 128

kernel_name = "hybrid_diffattn_pool_hgrn2_peer_adaln"

def rms_norm(x, g):
    xf = x.astype(jnp.float32)
    y = xf * lax.rsqrt(jnp.mean(xf * xf, axis=-1, keepdims=True) + RMS_EPS)
    return (y * g.astype(jnp.float32)).astype(x.dtype)

def lambda_init_fn(layer):
    return 0.8 - 0.6 * math.exp(-0.3 * layer)

def alibi_slopes():
    return jnp.asarray(np.array([2.0 ** (-8.0 * (h + 1) / ATT_HEADS) for h in range(ATT_HEADS)], dtype=np.float32))

def diff_attention(q, k, v, lam_qk, subln_g, layer):
    B, S, _ = q.shape
    lam_init = lambda_init_fn(layer)
    lq = lam_qk.astype(jnp.float32)
    lam = jnp.exp(jnp.sum(lq[0] * lq[1])) - jnp.exp(jnp.sum(lq[2] * lq[3])) + lam_init
    qh = q.reshape(B, S, ATT_HEADS, 2, ATT_DK).transpose(0, 3, 2, 1, 4)
    kh = k.reshape(B, S, ATT_HEADS, 2, ATT_DK).transpose(0, 3, 2, 1, 4)
    vh = v.reshape(B, S, ATT_HEADS, ATT_DV)
    slopes = alibi_slopes()[:, None, None]
    pos = jnp.arange(S)
    scale = ATT_DK ** -0.5
    outs = []
    for blk in range(S // ATT_BLOCK):
        q0 = blk * ATT_BLOCK
        kv_len = q0 + ATT_BLOCK
        qb = qh[:, :, :, q0:kv_len]
        kb = kh[:, :, :, :kv_len]
        vb = vh[:, :kv_len]
        s = jnp.einsum('bmhqd,bmhkd->bmhqk', qb, kb).astype(jnp.float32) * scale
        dist = (pos[q0:kv_len, None] - pos[None, :kv_len]).astype(jnp.float32)
        bias = jnp.where(dist[None] >= 0, -slopes * dist[None], MASK_VALUE)
        p = jax.nn.softmax(s + bias, axis=-1)
        a = p[:, 0] - lam * p[:, 1]
        outs.append(jnp.einsum('bhqk,bkhd->bqhd', a.astype(vb.dtype), vb))
    o = jnp.concatenate(outs, axis=1)
    o = rms_norm(o, subln_g) * (1.0 - lam_init)
    return o.reshape(B, S, ATT_V_WIDTH)

def multiscale_pool(p, pool_w, pool_scale):
    B, S, _ = p.shape
    cs = jnp.cumsum(p.astype(jnp.float32), axis=1)
    t1 = jnp.arange(1, S + 1)
    means = []
    for g, w in enumerate(POOL_WINDOWS):
        csg = cs[..., g * POOL_GW:(g + 1) * POOL_GW]
        shifted = jnp.pad(csg, ((0, 0), (w, 0), (0, 0)))[:, :S]
        count = jnp.minimum(t1, w).astype(jnp.float32)
        means.append((csg - shifted) / count[None, :, None])
    pooled = jnp.concatenate(means, axis=-1).astype(p.dtype) - p
    y = jnp.einsum('bsgc,gcd->bsgd', pooled.reshape(B, S, POOL_GROUPS, POOL_GW), pool_w)
    return y.reshape(B, S, POOL_WIDTH) * pool_scale

def hgrn2(q, f, i, g, lb, norm_g):
    B, S, _ = q.shape
    nc = S // HGRN_CHUNK

    def heads(t, d):
        return t.reshape(B, nc, HGRN_CHUNK, HGRN_HEADS, d).transpose(1, 0, 3, 2, 4).astype(jnp.float32)

    qh = heads(jax.nn.silu(q), HGRN_DK)
    lbh = lb.astype(jnp.float32).reshape(HGRN_HEADS, 1, HGRN_DK)
    logf = jnp.logaddexp(jnp.log(jnp.maximum(lbh, LB_FLOOR)),
                         jnp.log1p(-lbh) + jax.nn.log_sigmoid(heads(f, HGRN_DK)))
    kh = -jnp.expm1(logf)
    vh = heads(i, HGRN_DV)
    mask = jnp.tril(jnp.ones((HGRN_CHUNK, HGRN_CHUNK), dtype=bool))[:, :, None]

    def step(state, inp):
        qc, kc, lfc, vc = inp
        b = jnp.cumsum(lfc, axis=-2)
        diff = b[:, :, :, None, :] - b[:, :, None, :, :]
        decay = jnp.exp(jnp.where(mask, diff, MASK_VALUE))
        attn = jnp.einsum('bhtd,bhtsd,bhsd->bhts', qc, decay, kc)
        b_last = b[:, :, -1:, :]
        o = (jnp.einsum('bhts,bhsv->bhtv', attn, vc)
             + jnp.einsum('bhtd,bhdv->bhtv', qc * jnp.exp(b), state))
        state = (jnp.exp(b_last)[:, :, 0, :, None] * state
                 + jnp.einsum('bhsd,bhsv->bhdv', kc * jnp.exp(b_last - b), vc))
        return state, o

    s0 = jnp.zeros((B, HGRN_HEADS, HGRN_DK, HGRN_DV), jnp.float32)
    _, o = lax.scan(step, s0, (qh, kh, logf, vh))
    o = o.transpose(1, 0, 3, 2, 4).reshape(B, S, HGRN_HEADS, HGRN_DV).astype(q.dtype)
    o = rms_norm(o, norm_g) * jax.nn.silu(g.reshape(B, S, HGRN_HEADS, HGRN_DV))
    return o.reshape(B, S, HGRN_V_WIDTH)

def hybrid_mixer(h, layer, w_in, lam_qk, subln_g, pool_w, pool_scale, lb, hgrn_g, w_out):
    B, S, _ = h.shape
    z = h @ w_in
    points = []
    acc = 0
    for sz in IN_SIZES[:-1]:
        acc += sz
        points.append(acc)
    aq, ak, av, pp, hq, hf, hi, hg, zg = jnp.split(z, points, axis=-1)
    a_out = diff_attention(aq, ak, av, lam_qk, subln_g, layer)
    p_out = multiscale_pool(pp, pool_w, pool_scale)
    r_out = hgrn2(hq, hf, hi, hg, lb, hgrn_g)
    gates = jax.nn.sigmoid(zg).reshape(B, S, N_BRANCHES, D_MODEL)
    merged = gates[:, :, 0] * a_out + gates[:, :, 1] * p_out + gates[:, :, 2] * r_out
    return merged @ w_out

def peer_ffn(h, w_query, sub_keys, u_tab, v_tab):
    B, S, D = h.shape
    T = B * S
    xt = h.reshape(T, D)
    q = (xt @ w_query).reshape(T, PEER_HEADS, 2, PEER_DHALF)
    s = jnp.einsum('thpd,pkd->thpk', q, sub_keys).astype(jnp.float32)
    s_a, i_a = lax.top_k(s[:, :, 0], PEER_TOPK)
    s_b, i_b = lax.top_k(s[:, :, 1], PEER_TOPK)
    n_cand = PEER_TOPK * PEER_TOPK
    cand_s = (s_a[..., :, None] + s_b[..., None, :]).reshape(T, PEER_HEADS, n_cand)
    cand_i = (i_a[..., :, None] * PEER_NKEYS + i_b[..., None, :]).reshape(T, PEER_HEADS, n_cand)
    top_s, pos = lax.top_k(cand_s, PEER_TOPK)
    idx = jnp.take_along_axis(cand_i, pos, axis=-1)
    gate = jax.nn.softmax(top_s, axis=-1).astype(h.dtype)
    nb = T // PEER_TOKEN_BLOCK

    def apply(args):
        xb, ib, gb = args
        u = u_tab[ib]
        act = jax.nn.gelu(jnp.einsum('thkd,td->thk', u, xb), approximate=False)
        return jnp.einsum('thk,thkd->td', gb * act, v_tab[ib])

    out = lax.map(apply, (xt.reshape(nb, PEER_TOKEN_BLOCK, D),
                          idx.reshape(nb, PEER_TOKEN_BLOCK, PEER_HEADS, PEER_TOPK),
                          gate.reshape(nb, PEER_TOKEN_BLOCK, PEER_HEADS, PEER_TOPK)))
    return out.reshape(B, S, D)

def setup_inputs(seed: int = 0) -> dict:
    key = jax.random.key(seed)
    ks = jax.random.split(key, 19)
    D = D_MODEL

    def nrm(k, shape, scale):
        return jax.random.normal(k, shape, jnp.float32) * scale

    return {
        "x": nrm(ks[0], (BATCH, SEQ, D), 1.0),
        "c": nrm(ks[1], (BATCH, D), 1.0),
        "ada_w": nrm(ks[2], (DEPTH, D, 6 * D), 0.5 * D ** -0.5),
        "ada_b": nrm(ks[3], (DEPTH, 6 * D), 0.02),
        "norm_mix_g": 1.0 + nrm(ks[4], (DEPTH, D), 0.05),
        "w_in": nrm(ks[5], (DEPTH, D, IN_COLS), D ** -0.5),
        "diff_lambda": nrm(ks[6], (DEPTH, 4, ATT_DK), 0.1),
        "diff_subln_g": 1.0 + nrm(ks[7], (DEPTH, ATT_DV), 0.05),
        "pool_w": nrm(ks[8], (DEPTH, POOL_GROUPS, POOL_GW, POOL_GW), POOL_GW ** -0.5),
        "pool_scale": 1.0 + nrm(ks[9], (DEPTH, POOL_WIDTH), 0.05),
        "hgrn_lower_bounds": 1.0 + nrm(ks[10], (DEPTH, HGRN_K_WIDTH), 0.1),
        "hgrn_norm_g": 1.0 + nrm(ks[11], (DEPTH, HGRN_DV), 0.05),
        "w_out": nrm(ks[12], (DEPTH, D, D), D ** -0.5),
        "norm_ffn_g": 1.0 + nrm(ks[13], (DEPTH, D), 0.05),
        "peer_w_query": nrm(ks[14], (DEPTH, D, PEER_HEADS * PEER_DQ), D ** -0.5),
        "peer_sub_keys": nrm(ks[15], (DEPTH, 2, PEER_NKEYS, PEER_DHALF), PEER_DHALF ** -0.5),
        "peer_u": nrm(ks[16], (DEPTH, PEER_NEXPERTS, D), D ** -0.5),
        "peer_v": nrm(ks[17], (DEPTH, PEER_NEXPERTS, D), 1.0),
        "final_g": 1.0 + nrm(ks[18], (D,), 0.05),
    }

def reference(x, c, ada_w, ada_b, norm_mix_g, w_in, diff_lambda, diff_subln_g, pool_w, pool_scale,
              hgrn_lower_bounds, hgrn_norm_g, w_out, norm_ffn_g, peer_w_query, peer_sub_keys,
              peer_u, peer_v, final_g):
    p_lb = jax.nn.softmax(hgrn_lower_bounds.astype(jnp.float32), axis=0)
    lb_all = jnp.cumsum(p_lb, axis=0) - p_lb[0:1]
    c_act = jax.nn.silu(c)
    for l in range(DEPTH):
        ada = (c_act @ ada_w[l] + ada_b[l])[:, None, :]
        sh1, sc1, g1, sh2, sc2, g2 = jnp.split(ada, 6, axis=-1)
        h = rms_norm(x, norm_mix_g[l]) * (1.0 + sc1) + sh1
        x = x + g1 * hybrid_mixer(h, l, w_in[l], diff_lambda[l], diff_subln_g[l], pool_w[l],
                                  pool_scale[l], lb_all[l], hgrn_norm_g[l], w_out[l])
        h = rms_norm(x, norm_ffn_g[l]) * (1.0 + sc2) + sh2
        x = x + g2 * peer_ffn(h, peer_w_query[l], peer_sub_keys[l], peer_u[l], peer_v[l])
    return rms_norm(x, final_g)


_drawn_inputs = setup_inputs


def setup_inputs(seed=0):
    import zlib

    import numpy as np

    out = dict(_drawn_inputs(seed))
    spreads = {}
    factors = {'hgrn_lower_bounds': 26.098}
    for name, (base, spread) in spreads.items():
        noise = np.random.default_rng([zlib.crc32(name.encode()), seed]).standard_normal(out[name].shape)
        drawn = base * np.exp(spread * noise) if base else spread * noise
        out[name] = __import__('jax').numpy.asarray(drawn.astype(out[name].dtype))
    for name, factor in factors.items():
        out[name] = (out[name] * factor).astype(out[name].dtype)
    return out
```

```python
import math
from contextlib import ExitStack

import concourse.bass as bass
from concourse import mybir

F32 = mybir.dt.float32
U32 = mybir.dt.uint32
U8 = mybir.dt.uint8
I32 = mybir.dt.int32
ALU = mybir.AluOpType
ACT = mybir.ActivationFunctionType
AX = mybir.AxisListType.X

P = 128
D = 1024
T = 256
NT = T // P
DEPTH = 2
KC = D // P
HEADS = 8
PAIRS = HEADS // 2
SECT = 11
AQ, AK, AV, PP, HQ, HF, HI, HG, ZA, ZP, ZR = range(SECT)
LEVELS = 7
CROSS = LEVELS
WINDOWS = (2, 4, 8, 16)
EPS = 1e-6
FLOOR = 1e-20
MASKED = -1e33
NEXP = 16384
TOPK = 16
GROUP = 4
GROUPS = TOPK // GROUP
HGROUPS = NT * GROUPS
LGROUPS = HEADS * HGROUPS
CH = 256
ADA_CHUNKS = 6 * D // CH
ADA_PER_HEAD = ADA_CHUNKS // HEADS
BIG = 2.0 ** 32
LN_BIG = 32 * math.log(2.0)

B_Z = (0, 1, 2)
B_S0, B_S1, B_LA, B_LB, B_O = 3, 4, 5, 6, 7
B_Q, B_SC, B_ADA = 0, 1, (2, 3)
B_ACC = 4
UNITS = 6

MIX_CHAIN = 150
PEER_CHAIN = 99


def lambda_init(layer):
    return 0.8 - 0.6 * math.exp(-0.3 * layer)


def mixed(l):
    return (HEADS + 1) * l + 1


def dotted(l):
    return (LGROUPS + 1) * l + 1


def summed(l):
    return (LGROUPS + 4) * l + 4


class Chain:

    def __init__(self, eng, sem):
        self.eng, self.sem, self.base, self.n = eng, sem, 0, 0

    def __call__(self, ins):
        ins.then_inc(self.sem, 1)
        self.n += 1

    def sync(self):
        self.eng.wait_ge(self.sem, self.base + self.n)


def build(nc, x, c, ada_w, ada_b, norm_mix_g, w_in, diff_lambda, diff_subln_g, pool_w, pool_scale,
          hgrn_lower_bounds, hgrn_norm_g, w_out, norm_ffn_g, peer_w_query, peer_sub_keys,
          peer_u, peer_v, final_g, out):
    with ExitStack() as ctx:
        def sb(name, shape, dt=F32):
            return ctx.enter_context(nc.sbuf_tensor(name, shape, dt))

        def sem(name):
            return ctx.enter_context(nc.semaphore(name))

        PS = ctx.enter_context(nc.psum_tensor("PS", [P, 8, 512], F32))

        def bank(b):
            return PS[:, b, :]

        xs = sb("xs", [P, NT, D])
        tok = sb("tok", [P, NT, D])
        hT = sb("hT", [P, KC, T])
        ada = sb("ada", [P, 6, D])
        g2keep = sb("g2keep", [P, D])
        gain = sb("gain", [P, D])
        wbuf = [sb(f"wbuf{j}", [P, KC * SECT * P]) for j in range(2)]
        wz = [w[:].rearrange("p (k s n) -> p k s n", k=KC, s=SECT) for w in wbuf]
        wo_sb = wbuf[0][:, 0:KC * D].rearrange("p (k n) -> p k n", k=KC)
        ubuf = wbuf[0][:, 0:2 * GROUP * D].rearrange("p (b s d) -> p b s d", b=2, s=GROUP)
        vbuf = wbuf[1][:, 0:2 * GROUP * D].rearrange("p (b s d) -> p b s d", b=2, s=GROUP)
        ring = [sb(f"ring{j}", [P, KC * CH]) for j in range(2)]
        ringv = [r[:].rearrange("p (k n) -> p k n", k=KC) for r in ring]
        XD = ring[0][:].rearrange("p (l t) -> p l t", l=8)
        PW = 16 + T
        pt = [ring[1][:, i * 2 * PW:(i + 1) * 2 * PW].rearrange("p (h t) -> p h t", h=2) for i in range(2)]
        pooled = ring[1][:, 4 * PW:4 * PW + 2 * T].rearrange("p (h t) -> p h t", h=2)
        AT = ring[1][:, 4 * PW + 2 * T:4 * PW + 2 * T + 384].rearrange("p (b q) -> p b q", b=3)
        MSZ = 3328
        M = sb("M", [P, 2 * MSZ])

        def mreg(j, off, n):
            return M[:, j * MSZ + off:j * MSZ + off + n]

        qk = [mreg(j, 0, 512).rearrange("p (a t) -> p a t", a=2) for j in range(2)]
        hq = [mreg(j, 512, 256) for j in range(2)]
        e3 = [mreg(j, 768, 768).rearrange("p (a t) -> p a t", a=3) for j in range(2)]
        e4 = [mreg(j, 1536, 1024).rearrange("p (t a n) -> p t a n", t=2, a=4) for j in range(2)]
        vg = [mreg(j, 2560, 512).rearrange("p (t a n) -> p t a n", t=2, a=2) for j in range(2)]
        av = [mreg(j, 3072, 256).rearrange("p (t n) -> p t n", t=2) for j in range(2)]
        cb = M[:, 0:1024].rearrange("p (k n) -> p k n", k=KC)
        diag = M[:, 1024:2048].rearrange("p (b s n) -> p b s n", b=2, s=GROUP)
        qT = M[:, 2048:2560].rearrange("p (a t) -> p a t", a=2)
        keys_raw = M[:, 2560:2816].rearrange("p (a d) -> p a d", a=2)
        keysT = M[:, 2816:3072].rearrange("p (a d) -> p a d", a=2)
        wk = M[:, 3072:3200]
        cand = M[:, 3328:3584]
        cand2 = M[:, 3584:3840]
        oneh = M[:, 3840:4352].rearrange("p (a k n) -> p a k n", a=2, k=TOPK)
        pb = sb("pb", [P, 2, PW])
        pwt = sb("pwt", [P, 2, T])
        psc = sb("psc", [P, 2, P])
        ssc = sb("ssc", [P, 2, 384])
        am = sb("am", [P, 384])
        kk = sb("kk", [P, T])
        bs = sb("bs", [P, T])
        AH = sb("AH", [P, 3, P])
        ga = sb("ga", [P, 2, P])
        gr = sb("gr", [P, 2, P])
        spair = sb("spair", [P, 2, 2, P])
        osb = sb("osb", [P, 4, P])
        ident = sb("ident", [P, P])
        nd = sb("nd", [P, 384])
        lmask = sb("lmask", [P, LEVELS, P], U8)
        resetr = sb("resetr", [P, T])
        rc16 = sb("rc16", [P, 4, 16])
        rw = sb("rw", [P, 4])
        pm = sb("pm", [P, 4, 4])
        slopes = sb("slopes", [P, HEADS])
        iota16 = sb("iota16", [P, 16])
        mhalf = sb("mhalf", [P, 4])
        rows24 = sb("rows24", [24, P])
        col = sb("col", [P, 24])
        cact = sb("cact", [P, 8])
        lbp = sb("lbp", [P, 2, 8])
        lbm = sb("lbm", [P, 2, 8])
        oml = sb("oml", [P, 2, 8])
        dlt = sb("dlt", [P, 2, 8])
        small = sb("small", [P, 48])
        lamr = sb("lamr", [P, 256])
        subg = sb("subg", [P, P])
        ng = sb("ng", [P, P])
        lamn = sb("lamn", [P, 1])
        mx = sb("mx", [P, 4])
        sm = sb("sm", [P, 4])
        rl = sb("rl", [P, 2])
        ms = sb("ms", [P, 4])
        rsb = sb("rsb", [P, 4])
        rs = sb("rs", [P, 4])
        sv = sb("sv", [P, 2, TOPK])
        iu = sb("iu", [P, 2, TOPK], U32)
        idf = sb("idf", [P, 2, TOPK])
        ts = sb("ts", [P, TOPK])
        pos = sb("pos", [P, TOPK], U32)
        ab = sb("ab", [P, 2, TOPK], U32)
        abf = sb("abf", [P, 2, TOPK])
        red = sb("red", [P, 2, TOPK])
        idfl = sb("idfl", [P, TOPK])
        idx = [sb(f"idx{t}", [P, TOPK], U32) for t in range(2)]
        ge = sb("ge", [P, TOPK])
        rmx = sb("rmx", [P, 2])
        gate = [sb(f"gate{t}", [P, TOPK]) for t in range(2)]
        dots = [sb(f"dots{b}", [P, GROUP]) for b in range(2)]
        gel = [sb(f"gel{b}", [P, GROUP]) for b in range(2)]

        s_par, s_x, s_bias, s_gain = sem("s_par"), sem("s_x"), sem("s_bias"), sem("s_gain")
        s_small, s_keys, s_wo, s_pw = sem("s_small"), sem("s_keys"), sem("s_wo"), sem("s_pw")
        s_w = [sem("s_w0"), sem("s_w1")]
        s_r = [sem("s_r0"), sem("s_r1")]
        s_u = [sem("s_u0"), sem("s_u1")]
        s_v = [sem("s_v0"), sem("s_v1")]
        s_out = sem("s_out")
        s_const = sem("s_const")
        s_cstv = sem("s_cstv")
        s_vc = sem("s_vc")
        s_pc = sem("s_pc")
        s_colps = sem("s_colps")
        s_pcol = sem("s_pcol")
        s_pexp = sem("s_pexp")
        s_cb = sem("s_cb")
        s_chunk = sem("s_chunk")
        s_adaadd = sem("s_adaadd")
        s_gused = sem("s_gused")
        s_lamd, s_lame = sem("s_lamd"), sem("s_lame")
        s_smused = sem("s_smused")
        s_ms, s_rs = sem("s_ms"), sem("s_rs")
        s_tok = sem("s_tok")
        s_tp = sem("s_tp")
        s_hTa, s_hTd = sem("s_hTa"), sem("s_hTd")
        s_z, s_zev = sem("s_z"), sem("s_zev")
        s_F, s_ln = sem("s_F"), sem("s_ln")
        s_sc, s_mx, s_exp = sem("s_sc"), sem("s_mx"), sem("s_exp")
        s_D, s_E, s_X = sem("s_D"), sem("s_E"), sem("s_X")
        s_A, s_atp, s_at, s_avp = sem("s_A"), sem("s_atp"), sem("s_at"), sem("s_avp")
        s_lv, s_AH, s_op = sem("s_lv"), sem("s_AH"), sem("s_op")
        s_pooled, s_y = sem("s_pooled"), sem("s_y")
        s_mix = sem("s_mix")
        s_wod = sem("s_wod")
        s_kt, s_kte = sem("s_kt"), sem("s_kte")
        s_qev, s_psc, s_scfree = sem("s_qev"), sem("s_psc"), sem("s_scfree")
        s_rmx, s_rexp, s_route = sem("s_rmx"), sem("s_rexp"), sem("s_route")
        s_dot, s_gel, s_diag, s_vacc = sem("s_dot"), sem("s_gel"), sem("s_diag"), sem("s_vacc")
        s_peer = sem("s_peer")
        s_fin = sem("s_fin")

        w_in_v = [w_in[l].rearrange("(k p) (s n) -> k p s n", p=P, s=SECT) for l in range(DEPTH)]
        ada_w_v = [ada_w[l].rearrange("(k p) n -> p k n", p=P) for l in range(DEPTH)]
        wq_v = [peer_w_query[l].rearrange("(k p) n -> p k n", p=P) for l in range(DEPTH)]
        u_rows = peer_u.rearrange("l e d -> (l e) d")
        v_rows = peer_v.rearrange("l e d -> (l e) d")

        def brow(v, n):
            return v.rearrange("(o n) -> o n", o=1).to_broadcast([P, n])

        RB = [0, 12]
        R0 = ADA_CHUNKS
        R1 = R0 + 4 * HEADS

        def apart(eng):
            eng.nop(nofuse=True)

        block = ctx.enter_context(nc.Block())

        @block.sync
        def _(sp):
            sp.dma_start(rows24[0:8, :], c.rearrange("o (k n) -> (o k) n", k=8)).then_inc(s_par, 16)
            sp.dma_start(rows24[8:24, :], hgrn_lower_bounds.rearrange("l (k n) -> (l k) n", k=8)
                         ).then_inc(s_par, 16)

            def load_small(l):
                sp.dma_start(lamr[:], brow(diff_lambda[l].rearrange("a n -> (a n)"), 256)).then_inc(s_small, 16)
                sp.dma_start(subg[:], brow(diff_subln_g[l], P)).then_inc(s_small, 16)
                sp.dma_start(ng[:], brow(hgrn_norm_g[l], P)).then_inc(s_small, 16)

            def load_bias(l):
                sp.dma_start(ada[:].rearrange("p a n -> p (a n)"), brow(ada_b[l], 6 * D)).then_inc(s_bias, 16)

            def load_gain(v):
                sp.dma_start(gain[:], brow(v, D)).then_inc(s_gain, 16)

            def load_ada(l, col0, j):
                sp.dma_start(ringv[j], ada_w_v[l][:, :, bass.ds(col0, CH)]).then_inc(s_r[j], 16)

            def load_wq(l, h, j):
                sp.dma_start(ringv[j], wq_v[l][:, :, bass.ds(h * CH, CH)]).then_inc(s_r[j], 16)

            load_bias(0)
            load_ada(0, 0, 0)
            load_ada(0, CH, 1)
            load_gain(norm_mix_g[0])
            sp.dma_start(xs[:], x[0].rearrange("(t p) d -> p t d", p=P)).then_inc(s_x, 16)
            load_small(0)
            with sp.Fori(1, ADA_CHUNKS // 2) as i:
                for j in range(2):
                    sp.wait_ge(s_chunk, i * 2 + j - 1)
                    load_ada(0, i * (2 * CH) + j * CH, j)

            for l in range(DEPTH):
                def load_w(h, j):
                    for k in range(KC):
                        sp.dma_start(wz[j][:, k], w_in_v[l][k][:, :, bass.ds(h * P, P)]).then_inc(s_w[j], 16)

                def load_pool(g):
                    sp.dma_start(pwt[:], pool_w[l, bass.ds(g, 1), :, :].rearrange("o (h p) d -> p (o h) d", p=P)
                                 ).then_inc(s_pw, 16)
                    sp.dma_start(psc[:].rearrange("p a n -> p (a n)"),
                                 pool_scale[l:l + 1, bass.ds(g * T, T)].to_broadcast([P, T])).then_inc(s_pw, 16)

                if l:
                    sp.wait_ge(s_peer, l)
                load_w(0, 0)
                load_w(1, 1)
                load_pool(0)
                sp.wait_ge(s_gused, 2 * l + 1)
                load_gain(norm_ffn_g[l])
                with sp.Fori(1, PAIRS) as g:
                    for j in range(2):
                        sp.wait_ge(s_z, UNITS * HEADS * l + (g * 2 + (j - 1)) * UNITS)
                        load_w(g * 2 + j, j)
                    sp.wait_ge(s_mix, g * 2 + mixed(l))
                    load_pool(g)
                sp.wait_ge(s_z, UNITS * (HEADS * l + 7))
                sp.dma_start(wo_sb, w_out[l].rearrange("(k p) n -> p k n", p=P)).then_inc(s_wo, 16)
                sp.wait_ge(s_mix, mixed(l) + HEADS)
                load_wq(l, 0, 0)
                sp.dma_start(keys_raw, peer_sub_keys[l].rearrange("a k d -> k a d")).then_inc(s_keys, 16)
                sp.wait_ge(s_gused, 2 * l + 2)
                if l + 1 < DEPTH:
                    load_gain(norm_mix_g[l + 1])
                    sp.wait_ge(s_tok, 2 * l + 2)
                    load_bias(l + 1)
                    load_small(l + 1)
                    for i in range(ADA_PER_HEAD):
                        sp.wait_ge(s_chunk, R0 + i)
                        load_ada(l + 1, i * CH, (1 + i) % 2)
                    with sp.Fori(1, HEADS) as h:
                        sp.wait_ge(s_chunk, h * 4 + R0 - 1)
                        load_wq(l, h, 0)
                        for i in range(ADA_PER_HEAD):
                            sp.wait_ge(s_chunk, h * 4 + R0 + i)
                            load_ada(l + 1, h * (ADA_PER_HEAD * CH) + i * CH, (1 + i) % 2)
                else:
                    load_gain(final_g)
                    with sp.Fori(1, HEADS) as h:
                        sp.wait_ge(s_chunk, h + R1)
                        load_wq(l, h, 0)
            sp.wait_ge(s_fin, 1)
            sp.dma_start(out[0].rearrange("(t p) d -> p t d", p=P), tok[:]).then_inc(s_out, 16)
            sp.wait_ge(s_out, 16)

        @block.gpsimd
        def _(pool):
            pc = Chain(pool, s_pc)
            pc(nc.gpsimd.memset(ident[:], 0.0))
            pc(nc.gpsimd.memset(pb[:], 0.0))
            pc(nc.gpsimd.memset(mhalf[:], -0.5))
            pc(nc.gpsimd.memset(resetr[:], 1.0))
            iscr = hT[:].rearrange("p k t -> p (k t)").bitcast(I32)
            pc(nc.gpsimd.iota(iscr[:, 0:384], pattern=[[1, 384]], base=-P, channel_multiplier=-1))
            pc(nc.gpsimd.iota(iscr[:, 384:400], pattern=[[1, 16]], base=0, channel_multiplier=0))
            fm = tok[:].rearrange("p t d -> p (t d)")[:, 0:LEVELS * P].rearrange("p (l n) -> p l n", l=LEVELS)
            pc(nc.gpsimd.memset(fm, 1.0))
            pc.sync()
            pc(nc.gpsimd.affine_select(out=ident[:], in_=ident[:], compare_op=ALU.not_equal, fill=1.0, base=0,
                                       pattern=[[-1, P]], channel_multiplier=1))
            pc(nc.gpsimd.memset(resetr[:, 0:1], 0.0))
            pc(nc.gpsimd.memset(resetr[:, P:P + 1], 0.0))
            for i in range(LEVELS):
                m = 1 << i
                v = fm[:, i, :].rearrange("p (c b m) -> p c b m", c=2, m=m)
                nb = P // 2 // m
                pc.sync()
                pc(nc.gpsimd.affine_select(out=v, in_=v, compare_op=ALU.is_ge, fill=0.0, base=0,
                                           pattern=[[0, 2], [-2 * m, nb], [0, m]], channel_multiplier=1))
                pc.sync()
                last = nc.gpsimd.affine_select(out=v, in_=v, compare_op=ALU.is_ge, fill=0.0, base=m - 1,
                                               pattern=[[0, 2], [2 * m, nb], [0, m]], channel_multiplier=-1)
                if i < LEVELS - 1:
                    pc(last)
            last.then_inc(s_const, 1)
            pool.wait_ge(s_cstv, 1)
            for a in (0, 256):
                n = 256 if a == 0 else 128
                off = 0 if a == 0 else 128
                nc.gpsimd.affine_select(out=nd[:, a:a + n], in_=nd[:, a:a + n], compare_op=ALU.is_ge, fill=MASKED,
                                        base=P - off, pattern=[[-1, n]], channel_multiplier=1).then_inc(s_const, 1)

            def rsqrt(k, n, width):
                pool.wait_ge(s_ms, k + 1)
                apart(pool)
                pc(nc.gpsimd.tensor_scalar(rsb[:, 0:n], ms[:, 0:n], 1.0 / width, EPS, ALU.mult, ALU.add))
                pc.sync()
                nc.gpsimd.tensor_tensor(rs[:, 0:n], rsb[:, 0:n], mhalf[:, 0:n], ALU.pow).then_inc(s_rs, 1)

            NR = HEADS + 2
            for l in range(DEPTH):
                rsqrt(NR * l, NT, D)
                start = pc.n
                with pool.Fori(0, HEADS) as h:
                    pc.base, pc.n = h + start, 0
                    rsqrt(h + (NR * l + 1), 4, P)
                pc.base, pc.n = 0, start + HEADS
                rsqrt(NR * l + HEADS + 1, NT, D)

                def gather_u(h, gi):
                    t, q = gi // GROUPS, gi % GROUPS
                    if q == 0:
                        pool.wait_ge(s_route, h * NT + (2 * HEADS * l + t + 1))
                    if l or gi or not isinstance(h, int) or h:
                        pool.wait_ge(s_dot, h * HGROUPS + (dotted(l) + gi - 1))
                    apart(pool)
                    for s in range(GROUP):
                        k = q * GROUP + s
                        nc.gpsimd.indirect_dma_start(
                            out=ubuf[:, gi % 2, s, :], out_offset=None, in_=u_rows,
                            in_offset=bass.IndirectOffsetOnAxis(ap=idx[t][:, k:k + 1], axis=0)).then_inc(s_u[gi % 2], 16)

                def gather_v(h, gi):
                    t, q = gi // GROUPS, gi % GROUPS
                    pool.wait_ge(s_vacc, h * HGROUPS + (summed(l) + gi - 1))
                    apart(pool)
                    for s in range(GROUP):
                        k = q * GROUP + s
                        nc.gpsimd.indirect_dma_start(
                            out=vbuf[:, gi % 2, s, :], out_offset=None, in_=v_rows,
                            in_offset=bass.IndirectOffsetOnAxis(ap=idx[t][:, k:k + 1], axis=0)).then_inc(s_v[gi % 2], 16)

                def head(h, more):
                    for gi in range(HGROUPS):
                        if gi + 1 < HGROUPS:
                            gather_u(h, gi + 1)
                        elif more:
                            gather_u(h + 1, 0)
                        gather_v(h, gi)

                gather_u(0, 0)
                with pool.Fori(0, HEADS - 1) as h:
                    head(h, True)
                head(HEADS - 1, False)
            rsqrt(NR * DEPTH, NT, D)

        @block.scalar
        def _(act):
            act.wait_ge(s_pcol, 1)
            nc.scalar.activation(small[:, 0:8], col[:, 0:8], ACT.Exp, scale=-1.0)
            nc.scalar.activation(lbp[:].rearrange("p a n -> p (a n)"), small[:, 8:24], ACT.Exp).then_inc(s_pexp, 1)

            def evac_hT(n):
                for b in range(2):
                    act.wait_ge(s_tp, 4 * n + b + 1)
                    nc.scalar.activation(hT[:, 2 * b:2 * b + 2, :].rearrange("p k t -> p (k t)"), bank(b),
                                         ACT.Copy).then_inc(s_hTa, 1)

            for l in range(DEPTH):
                act.wait_ge(s_lamd, l + 1)
                nc.scalar.activation(small[:, 26:28], small[:, 24:26], ACT.Exp).then_inc(s_lame, 1)
                evac_hT(3 * l)
                H0 = HEADS * l

                def unit_ready(n, u):
                    act.wait_ge(s_z, (n + H0) * UNITS + (u + 1))

                def evac(n, j, u, g=None):
                    b = bank(B_Z[u % 3])
                    unit_ready(n, u)
                    if u == 0:
                        nc.scalar.mul(qk[j][:, 0, :], b[:, 0:T], 0.125)
                        nc.scalar.activation(qk[j][:, 1, :], b[:, T:2 * T], ACT.Copy).then_inc(s_zev, 1)
                    elif u == 1:
                        nc.scalar.activation(hq[j], b[:, 0:T], ACT.Copy)
                        nc.scalar.activation(e3[j][:, 0:2, :].rearrange("p a t -> p (a t)"), b, ACT.Exp, scale=-1.0)
                        nc.scalar.activation(e3[j][:, 2, :], b[:, T:2 * T], ACT.Exp).then_inc(s_zev, 1)
                    elif u == 2:
                        nc.scalar.activation(pb[:, j, 16:16 + T], b[:, 0:T], ACT.Copy).then_inc(s_zev, 1)
                    elif u in (3, 4):
                        nc.scalar.activation(vg[j][:, u - 3].rearrange("p a n -> p (a n)"), b[:, 0:256], ACT.Copy)
                        nc.scalar.activation(e4[j][:, u - 3, 0:3].rearrange("p a n -> p (a n)"), b[:, 128:512],
                                             ACT.Exp, scale=-1.0).then_inc(s_zev, 1)
                    else:
                        bv = b.rearrange("p (t a n) -> p t a n", t=2, a=2)
                        nc.scalar.activation(av[j], bv[:, :, 0, :], ACT.Copy)
                        nc.scalar.activation(e4[j][:, :, 3, :], bv[:, :, 1, :], ACT.Exp, scale=-1.0).then_inc(s_zev, 1)

                def step(n, m, jm, g):
                    jn = 1 - jm
                    if n is not None:
                        if not (isinstance(n, int) and n < 2 and l == 0):
                            act.wait_ge(s_mix, n + (mixed(l) - 1))
                        evac(n, jn, 0)
                    act.wait_ge(s_F, m + (H0 + 1))
                    nc.scalar.activation(XD[:, 3, :], XD[:, 0, :], ACT.Ln).then_inc(s_ln, 1)
                    if n is not None:
                        evac(n, jn, 1)
                    act.wait_ge(s_mx, m + (H0 + 1))
                    for t in range(2):
                        for a in range(2):
                            cols = slice(256, 384) if t == 0 else slice(0, 256)
                            i = nc.scalar.activation(ssc[:, a, cols], ssc[:, a, cols], ACT.Exp,
                                                     bias=mx[:, 2 * t + a:2 * t + a + 1],
                                                     accum_out=sm[:, 2 * t + a:2 * t + a + 1])
                    i.then_inc(s_exp, 1)
                    act.wait_ge(s_D, m + (H0 + 1))
                    xf = XD.rearrange("p l t -> p (l t)")
                    nc.scalar.activation(xf, xf, ACT.Exp).then_inc(s_E, 1)
                    if n is not None:
                        if jn == 0:
                            act.wait_ge(s_pooled, g + (PAIRS * l + 1))
                        evac(n, jn, 2)
                        for u in range(3, UNITS):
                            evac(n, jn, u)

                if l:
                    act.wait_ge(s_mix, mixed(l) - 1)
                for u in range(UNITS):
                    evac(0, 0, u)
                with act.Fori(0, PAIRS - 1) as g:
                    step(g * 2 + 1, g * 2, 0, g)
                    step(g * 2 + 2, g * 2 + 1, 1, g)
                step(HEADS - 1, HEADS - 2, 0, PAIRS - 1)
                step(None, HEADS - 1, 1, PAIRS - 1)
                evac_hT(3 * l + 1)

                act.wait_ge(s_kt, l + 1)
                nc.scalar.activation(keysT.rearrange("p a d -> p (a d)"), bank(B_SC)[:, 0:256],
                                     ACT.Copy).then_inc(s_kte, 1)
                evac_hT(3 * l + 2)
                per = 4 if l + 1 < DEPTH else 1
                r0 = R0 if l + 1 < DEPTH else R1

                def q_evac(h):
                    act.wait_ge(s_chunk, h * per + (r0 + 1))
                    nc.scalar.activation(qT.rearrange("p a t -> p (a t)"), bank(B_Q), ACT.Copy).then_inc(s_qev, 1)

                def route_exp(h, t):
                    act.wait_ge(s_rmx, h * NT + (2 * HEADS * l + t + 1))
                    nc.scalar.activation(ge[:], ts[:], ACT.Exp, bias=rmx[:, 0:1],
                                         accum_out=rmx[:, 1:2]).then_inc(s_rexp, 1)

                def head(h, more):
                    for gi in range(HGROUPS):
                        act.wait_ge(s_dot, h * HGROUPS + (dotted(l) + gi + 1))
                        nc.scalar.activation(gel[gi % 2][:], dots[gi % 2][:], ACT.Gelu).then_inc(s_gel, 1)
                        if gi == 2:
                            route_exp(h, 1)
                            if more:
                                q_evac(h + 1)
                        if gi == GROUPS + 2 and more:
                            route_exp(h + 1, 0)

                q_evac(0)
                route_exp(0, 0)
                with act.Fori(0, HEADS - 1) as h:
                    head(h, True)
                head(HEADS - 1, False)

        @block.tensor
        def _(pe):
            mm = nc.tensor.matmul

            pe.wait_ge(s_const, 1)
            pe.wait_ge(s_par, 32)
            nc.tensor.transpose(bank(B_Q)[:, 0:24], rows24[:], ident[0:24, 0:24]).then_inc(s_colps, 1)

            def ada_chunk(j, b):
                for k in range(KC):
                    i = mm(bank(b)[:, 0:CH], cb[:, k, :], ringv[j][:, k, :], start=(k == 0), stop=(k == KC - 1))
                i.then_inc(s_chunk, 1)

            pe.wait_ge(s_cb, 1)
            for j in range(2):
                pe.wait_ge(s_r[j], 16)
                ada_chunk(j, B_ADA[j])
            with pe.Fori(1, ADA_CHUNKS // 2) as i:
                for j in range(2):
                    pe.wait_ge(s_r[j], i * 16 + 16)
                    pe.wait_ge(s_adaadd, i * 2 + j - 1)
                    ada_chunk(j, B_ADA[j])

            def transpose_tok():
                for b in range(4):
                    for k in (2 * b, 2 * b + 1):
                        for t in range(NT):
                            o = (k % 2) * T + t * P
                            i = nc.tensor.transpose(bank(b)[:, o:o + P], tok[:, t, k * P:(k + 1) * P], ident[:])
                    i.then_inc(s_tp, 1)

            def hT_ready(n):
                pe.wait_ge(s_hTa, 2 * (n + 1))
                pe.wait_ge(s_hTd, 2 * (n + 1))

            for l in range(DEPTH):
                H0 = HEADS * l
                pe.wait_ge(s_tok, 2 * l + 1)
                transpose_tok()
                hT_ready(3 * l)

                def project(n, j, u):
                    b = bank(B_Z[u % 3])
                    if u == 0:
                        pe.wait_ge(s_w[j], (n - j) * (64) + (64 * H0 + 128))
                    if not (isinstance(n, int) and n == 0 and u < 3):
                        pe.wait_ge(s_zev, (n + H0) * UNITS + (u - 2))
                    elif l:
                        pe.wait_ge(s_zev, H0 * UNITS)
                    if u < 3:
                        for i, s in enumerate(((AQ, AK), (HQ, HF), (PP,))[u]):
                            for k in range(KC):
                                ins = mm(b[:, i * T:(i + 1) * T], wz[j][:, k, s, :], hT[:, k, :],
                                         start=(k == 0), stop=(k == KC - 1))
                    elif u in (3, 4):
                        t = u - 3
                        for k in range(KC):
                            ins = mm(b, hT[:, k, t * P:(t + 1) * P], wz[j][:, k, HI:ZP + 1, :],
                                     start=(k == 0), stop=(k == KC - 1))
                    else:
                        for t in range(NT):
                            for k in range(KC):
                                ins = mm(b[:, t * 256:(t + 1) * 256], hT[:, k, t * P:(t + 1) * P],
                                         wz[j][:, k, AV:ZR + 1:ZR - AV, :], start=(k == 0), stop=(k == KC - 1))
                    ins.then_inc(s_z, 1)

                def step(n, m, jm, g):
                    jn = 1 - jm
                    one = H0 + 1

                    def proj(u):
                        if n is not None:
                            project(n, jn, u)

                    proj(0)
                    pe.wait_ge(s_mix, m + mixed(l))
                    pe.wait_ge(s_zev, (m + H0) * UNITS + 1)
                    for a, b in enumerate((B_S0, B_S1)):
                        r = slice(64 * a, 64 * a + 64)
                        mm(bank(b)[:, 0:256], qk[jm][r, 0, P:T], qk[jm][r, 1, :], start=True, stop=True)
                        i = mm(bank(b)[:, 256:384], qk[jm][r, 0, 0:P], qk[jm][r, 1, 0:P], start=True, stop=True)
                    i.then_inc(s_sc, 1)
                    proj(1)
                    pe.wait_ge(s_X, m + one)
                    for lv in range(LEVELS + 1):
                        if lv == CROSS:
                            i = mm(bank(B_LB)[:, 384:512], XD[:, lv, 0:P], XD[:, lv, P:T], start=True, stop=True)
                            continue
                        b, o = (B_LA, lv * P) if lv < 4 else (B_LB, (lv - 4) * P)
                        for ck in range(2):
                            right = XD[:, lv, ck * P:(ck + 1) * P].rearrange(
                                "p (b w m) -> p b w m", w=2, m=1 << lv)[:, :, 1, :]
                            mm(bank(b)[:, o + 64 * ck:o + 64 * ck + 64], XD[:, lv, ck * P:(ck + 1) * P], right,
                               start=True, stop=True)
                    for ck in range(2):
                        i = mm(bank(B_O)[:, ck * P:(ck + 1) * P], kk[:, ck * P:(ck + 1) * P],
                               hq[jm][:, ck * P:(ck + 1) * P], start=True, stop=True)
                    i.then_inc(s_lv, 1)
                    proj(2)
                    pe.wait_ge(s_A, m + one)
                    for b in range(3):
                        i = nc.tensor.transpose(bank(B_S0)[:, b * P:(b + 1) * P], am[:, b * P:(b + 1) * P], ident[:])
                    i.then_inc(s_atp, 1)
                    proj(3)
                    pe.wait_ge(s_at, m + one)
                    mm(bank(B_S1)[:, 0:P], AT[:, 2, :], av[jm][:, 0, :], start=True, stop=True)
                    mm(bank(B_S1)[:, P:2 * P], AT[:, 0, :], av[jm][:, 0, :], start=True, stop=False)
                    mm(bank(B_S1)[:, P:2 * P], AT[:, 1, :], av[jm][:, 1, :], start=False, stop=True
                       ).then_inc(s_avp, 1)
                    proj(4)
                    pe.wait_ge(s_AH, m + one)
                    mm(bank(B_O)[:, 0:P], AH[:, 0, :], vg[jm][:, 0, 0, :], start=True, stop=True)
                    mm(bank(B_O)[:, P:2 * P], AH[:, 1, :], vg[jm][:, 1, 0, :], start=True, stop=False)
                    mm(bank(B_O)[:, P:2 * P], AH[:, 2, :], vg[jm][:, 0, 0, :], start=False, stop=True
                       ).then_inc(s_op, 1)
                    if jm == 1:
                        pe.wait_ge(s_pooled, g + (PAIRS * l + 1))
                        pe.wait_ge(s_pw, g * 32 + (32 * PAIRS * l + 32))
                        for t in range(NT):
                            for hf in range(2):
                                i = mm(bank(B_LA)[:, t * T:(t + 1) * T], pooled[:, hf, t * P:(t + 1) * P],
                                       pwt[:, hf, :], start=(hf == 0), stop=(hf == 1))
                        i.then_inc(s_y, 1)
                    proj(5)

                for u in range(UNITS):
                    project(0, 0, u)
                with pe.Fori(0, PAIRS - 1) as g:
                    step(g * 2 + 1, g * 2, 0, g)
                    step(g * 2 + 2, g * 2 + 1, 1, g)
                step(HEADS - 1, HEADS - 2, 0, PAIRS - 1)
                step(None, HEADS - 1, 1, PAIRS - 1)

                pe.wait_ge(s_mix, mixed(l) + HEADS)
                transpose_tok()
                hT_ready(3 * l + 1)
                pe.wait_ge(s_wo, 16 * (l + 1))
                for t in range(NT):
                    for hf in range(2):
                        for k in range(KC):
                            i = mm(bank(B_ACC + 2 * t + hf), hT[:, k, t * P:(t + 1) * P],
                                   wo_sb[:, k, hf * 512:(hf + 1) * 512], start=(k == 0), stop=(k == KC - 1))
                    i.then_inc(s_wod, 1)

                pe.wait_ge(s_keys, 16 * (l + 1))
                for a in range(2):
                    i = nc.tensor.transpose(bank(B_SC)[:, a * P:(a + 1) * P], keys_raw[:, a, :], ident[:])
                i.then_inc(s_kt, 1)
                pe.wait_ge(s_kte, l + 1)
                pe.wait_ge(s_tok, 2 * l + 2)
                transpose_tok()
                hT_ready(3 * l + 2)
                more_ada = l + 1 < DEPTH

                def queries(h):
                    n = (h * 2 + (R0 // 2 + 1)) if more_ada else (h + (R1 // 2 + 1))
                    pe.wait_ge(s_r[0], n * 16)
                    for a in range(2):
                        for k in range(KC):
                            i = mm(bank(B_Q)[:, a * T:(a + 1) * T], ringv[0][:, k, a * P:(a + 1) * P], hT[:, k, :],
                                   start=(k == 0), stop=(k == KC - 1))
                    i.then_inc(s_chunk, 1)

                def key_scores(h):
                    pe.wait_ge(s_qev, h + (HEADS * l + 1))
                    if not (isinstance(h, int) and h == 0 and l == 0):
                        pe.wait_ge(s_scfree, h + HEADS * l)
                    for t in range(NT):
                        for a in range(2):
                            o = (t * 2 + a) * P
                            i = mm(bank(B_SC)[:, o:o + P], qT[:, a, t * P:(t + 1) * P], keysT[:, a, :],
                                   start=True, stop=True)
                    i.then_inc(s_psc, 1)

                def expert_sum(h, gi, last=False):
                    t = gi // GROUPS
                    pe.wait_ge(s_diag, h * HGROUPS + (LGROUPS * l + gi + 1))
                    pe.wait_ge(s_v[gi % 2], h * (16 * HGROUPS * GROUP // 2)
                               + 64 * (LGROUPS // 2 * l + gi // 2 + 1))
                    for s in range(GROUP):
                        for hf in range(2):
                            i = mm(bank(B_ACC + 2 * t + hf), diag[:, gi % 2, s, :],
                                   vbuf[:, gi % 2, s, hf * 512:(hf + 1) * 512], start=False,
                                   stop=(last and s == GROUP - 1), skip_group_check=True)
                    i.then_inc(s_vacc, 1)

                def head(h, more):
                    for gi in range(HGROUPS):
                        if more_ada and gi < ADA_PER_HEAD:
                            j = (1 + gi) % 2
                            n = h * (2 if j == 1 else 2) + (R0 // 2 + (1 if gi == 0 else 2))
                            pe.wait_ge(s_r[j], n * 16)
                            pe.wait_ge(s_adaadd, h * ADA_PER_HEAD + (ADA_CHUNKS + gi))
                            ada_chunk(j, B_ADA[gi % 2])
                        if more and gi == ADA_PER_HEAD:
                            key_scores(h + 1)
                        expert_sum(h, gi, not more and gi % GROUPS == GROUPS - 1)
                        if more and gi == ADA_PER_HEAD - 1:
                            queries(h + 1)

                queries(0)
                key_scores(0)
                pe.wait_ge(s_cb, l + 2)
                for b in range(4):
                    i = mm(bank(B_ACC + b), diag[:, 1, GROUP - 1, :], hT[:, 0:2, :], start=True, stop=False,
                           skip_group_check=True)
                    i.then_inc(s_vacc, 1)
                with pe.Fori(0, HEADS - 1) as h:
                    head(h, True)
                head(HEADS - 1, False)

        @block.vector
        def _(dve):
            v = nc.vector
            ch = Chain(dve, s_vc)

            def copy(o, i):
                return v.tensor_copy(o, i)

            def sts(o, a, s1, s2, op0, op1):
                return v.tensor_scalar(o, a, s1, s2, op0, op1)

            def stt(o, a, s, b, op0, op1):
                return v.scalar_tensor_tensor(out=o, in0=a, scalar=s, in1=b, op0=op0, op1=op1)

            def dot(o, a, b, acc):
                return v.tensor_tensor_reduce(out=o, in0=a, in1=b, scale=1.0, scalar=0.0, op0=ALU.mult,
                                              op1=ALU.add, accum_out=acc)

            for h in range(HEADS):
                ch(v.memset(slopes[:, h:h + 1], 2.0 ** -(h + 1)))
            ch(v.memset(pm[:], 0.0))
            ch.sync()
            for g in range(4):
                ch(v.memset(pm[:, g, 0:g + 1], 1.0))
                ch(v.memset(rw[:, g:g + 1], 1.0 / WINDOWS[g]))
            dve.wait_ge(s_const, 1)
            iscr = hT[:].rearrange("p k t -> p (k t)").bitcast(I32)
            fm = tok[:].rearrange("p t d -> p (t d)")[:, 0:LEVELS * P].rearrange("p (l n) -> p l n", l=LEVELS)
            ch(copy(lmask[:], fm))
            ch(copy(iota16[:], iscr[:, 384:400]))
            ch(copy(nd[:, 256:384], iscr[:, 128:256]))
            copy(nd[:, 0:256], iscr[:, 0:256]).then_inc(s_cstv, 1)
            ch.sync()
            for g in range(4):
                ch(sts(rc16[:, g, :], iota16[:], 1.0, float(WINDOWS[g]), ALU.add, ALU.min))
            ch.sync()
            ch(v.reciprocal(rc16[:], rc16[:]))
            dve.wait_ge(s_colps, 1)
            ch(copy(col[:], bank(B_Q)[:, 0:24]))
            ch.sync()
            ch(v.tensor_tensor(small[:, 32:40], col[:, 8:16], col[:, 16:24], ALU.max))
            ch.sync()
            ch(v.tensor_tensor(small[:, 8:16], col[:, 8:16], small[:, 32:40], ALU.subtract))
            v.tensor_tensor(small[:, 16:24], col[:, 16:24], small[:, 32:40], ALU.subtract).then_inc(s_pcol, 1)
            dve.wait_ge(s_pexp, 1)
            ch(sts(small[:, 0:8], small[:, 0:8], 1.0, None, ALU.add, ALU.bypass))
            ch(v.tensor_tensor(small[:, 32:40], lbp[:, 0, :], lbp[:, 1, :], ALU.add))
            ch.sync()
            ch(v.reciprocal(small[:, 0:8], small[:, 0:8]))
            ch(v.reciprocal(small[:, 32:40], small[:, 32:40]))
            ch.sync()
            ch(v.tensor_tensor(cact[:], col[:, 0:8], small[:, 0:8], ALU.mult))
            ch(v.tensor_tensor(lbp[:], lbp[:], small[:, 32:40].unsqueeze(1).to_broadcast([P, 2, 8]), ALU.mult))
            ch.sync()
            copy(cb, cact[:].unsqueeze(2).to_broadcast([P, KC, P])).then_inc(s_cb, 1)
            ch(v.tensor_tensor(lbp[:, 1, :], lbp[:, 0, :], lbp[:, 1, :], ALU.add))
            ch.sync()
            ch(v.tensor_tensor(lbp[:, 1, :], lbp[:, 1, :], lbp[:, 0, :], ALU.subtract))
            ch.sync()
            ch(v.memset(lbp[:, 0, :], 0.0))
            ch.sync()
            ch(sts(lbm[:], lbp[:], FLOOR, None, ALU.max, ALU.bypass))
            ch(sts(oml[:], lbp[:], -1.0, 1.0, ALU.mult, ALU.add))
            ch.sync()
            ch(v.tensor_tensor(dlt[:], lbm[:], lbp[:], ALU.subtract))

            def add_ada(r, b, col0):
                dve.wait_ge(s_chunk, r + 1)
                a = ada[:].rearrange("p a n -> p (a n)")[:, bass.ds(col0, CH)]
                v.tensor_tensor(a, bank(b)[:, 0:CH], a, ALU.add).then_inc(s_adaadd, 1)

            dve.wait_ge(s_bias, 16)
            with dve.Fori(0, ADA_CHUNKS // 2) as i:
                for j in range(2):
                    add_ada(i * 2 + j, B_ADA[j], i * (2 * CH) + j * CH)

            def normed(n, k, sh, sc):
                dve.wait_ge(s_gain, 16 * (n + 1))
                ch.sync()
                stt(ada[:, sc, :], ada[:, sc, :], 1.0, gain[:], ALU.add, ALU.mult).then_inc(s_gused, 1)
                ch(dot(tok[:, 0, :], xs[:, 0, :], xs[:, 0, :], ms[:, 0:1]))
                dot(tok[:, 1, :], xs[:, 1, :], xs[:, 1, :], ms[:, 1:2]).then_inc(s_ms, 1)
                dve.wait_ge(s_rs, k + 1)
                dve.wait_ge(s_gused, n + 1)
                for t in range(NT):
                    ch(stt(tok[:, t, :], xs[:, t, :], rs[:, t:t + 1], ada[:, sc, :], ALU.mult, ALU.mult))
                ch.sync()
                ch(v.tensor_tensor(tok[:, 0, :], tok[:, 0, :], ada[:, sh, :], ALU.add))
                return v.tensor_tensor(tok[:, 1, :], tok[:, 1, :], ada[:, sh, :], ALU.add)

            def evac_hT(n):
                for b in (2, 3):
                    dve.wait_ge(s_tp, 4 * n + b + 1)
                    copy(hT[:, 2 * b:2 * b + 2, :].rearrange("p k t -> p (k t)"), bank(b)).then_inc(s_hTd, 1)

            NR = HEADS + 2
            dve.wait_ge(s_x, 16)
            dve.wait_ge(s_const, 3)
            dve.wait_ge(s_adaadd, ADA_CHUNKS)
            for l in range(DEPTH):
                H0 = HEADS * l
                dve.wait_ge(s_small, 48 * (l + 1))
                ch(dot(lamr[:, 0:64], lamr[:, 0:64], lamr[:, 64:128], small[:, 24:25]))
                dot(lamr[:, 128:192], lamr[:, 128:192], lamr[:, 192:256], small[:, 25:26]).then_inc(s_lamd, 1)
                dve.wait_ge(s_lame, l + 1)
                ch(stt(lamn[:], small[:, 27:28], -lambda_init(l), small[:, 26:27], ALU.add, ALU.subtract))
                sts(subg[:], subg[:], 1.0 - lambda_init(l), None, ALU.mult, ALU.bypass).then_inc(s_mix, 1)
                normed(2 * l, NR * l, 0, 1).then_inc(s_tok, 1)
                evac_hT(3 * l)

                def lview(a, lv, ck2=True):
                    return a.rearrange("p (b w m) -> p b w m", w=2, m=1 << lv)

                def step(h, j, g, up):
                    one = H0 + 1
                    mg = tok[:, :, bass.ds(h * P, P)]
                    if j == 1:
                        dve.wait_ge(s_zev, h * UNITS + (H0 * UNITS + 3))
                        src = pb[:]
                        for k in range(4):
                            d, lo = 1 << k, (2 << k) - 1
                            dst = pt[k % 2]
                            ch(stt(dst[:, :, lo:PW], src[:, :, lo - d:PW - d], pm[:, bass.ds(g, 1), k:k + 1].rearrange("p a b -> p (a b)"),
                                   src[:, :, lo:PW], ALU.mult, ALU.add))
                            ch.sync()
                            src = dst
                        p0 = pb[:, :, 16:32]
                        ch(stt(pooled[:, :, 16:T], src[:, :, 32:PW], rw[:, bass.ds(g, 1)], pb[:, :, 32:PW],
                               ALU.mult, ALU.subtract))
                        ch(v.tensor_tensor(pooled[:, :, 0:16], src[:, :, 16:32],
                                           rc16[:, bass.ds(g, 1), :].to_broadcast([P, 2, 16]), ALU.mult))
                        ch.sync()
                        v.tensor_tensor(pooled[:, :, 0:16], pooled[:, :, 0:16], p0, ALU.subtract).then_inc(s_pooled, 1)
                    dve.wait_ge(s_zev, h * UNITS + (H0 * UNITS + 2))
                    e = e3[j].rearrange("p a t -> p (a t)")
                    ch(sts(e, e, 1.0, None, ALU.add, ALU.bypass))
                    ch.sync()
                    ch(v.reciprocal(e, e))
                    ch.sync()
                    ch(sts(XD[:, 2, :], e3[j][:, 1, :], oml[:, l, bass.ds(h, 1)], lbm[:, l, bass.ds(h, 1)], ALU.mult, ALU.add))
                    ch(sts(kk[:], e3[j][:, 2, :], oml[:, l, bass.ds(h, 1)], dlt[:, l, bass.ds(h, 1)], ALU.mult, ALU.subtract))
                    ch(v.tensor_tensor(hq[j], hq[j], e3[j][:, 0, :], ALU.mult))
                    ch.sync()
                    ch(sts(XD[:, 1, :], XD[:, 2, :], 1.0 / BIG, BIG, ALU.is_lt, ALU.mult))
                    ch.sync()
                    stt(XD[:, 0, :], XD[:, 1, :], 1.0, XD[:, 2, :], ALU.add, ALU.mult).then_inc(s_F, 1)
                    dve.wait_ge(s_sc, h + one)
                    for a, b in enumerate((B_S0, B_S1)):
                        ch(stt(ssc[:, a, :], nd[:], slopes[:, bass.ds(h, 1)], bank(b)[:, 0:384], ALU.mult, ALU.add))
                    ch.sync()
                    ch(v.tensor_reduce(mx[:, 0:2], ssc[:, :, 256:384], AX, ALU.max))
                    ch(v.tensor_reduce(mx[:, 2:4], ssc[:, :, 0:256], AX, ALU.max))
                    ch.sync()
                    sts(mx[:], mx[:], -1.0, None, ALU.mult, ALU.bypass).then_inc(s_mx, 1)
                    dve.wait_ge(s_ln, h + one)
                    ch(stt(XD[:, 3, :], XD[:, 1, :], -LN_BIG / BIG, XD[:, 3, :], ALU.mult, ALU.add))
                    ch.sync()
                    ch(v.tensor_tensor_scan(bs[:], resetr[:], XD[:, 3, :], 0.0, ALU.mult, ALU.add))
                    ch.sync()
                    for lv in range(LEVELS):
                        m = 1 << lv
                        dv, bv = lview(XD[:, lv, :], lv), lview(bs[:], lv)
                        mid = bv[:, :, 0, m - 1:m].to_broadcast([P, P // m, m])
                        ch(v.tensor_tensor(dv[:, :, 1, :], bv[:, :, 1, :], mid, ALU.subtract))
                        ch(v.tensor_tensor(dv[:, :, 0, :], mid, bv[:, :, 0, :], ALU.subtract))
                    ch(copy(XD[:, CROSS, P:T], bs[:, P:T]))
                    v.tensor_tensor(XD[:, CROSS, 0:P], bs[:, P - 1:P].to_broadcast([P, P]), bs[:, 0:P],
                                    ALU.subtract).then_inc(s_D, 1)
                    dve.wait_ge(s_exp, h + one)
                    ch(v.reciprocal(sm[:], sm[:]))
                    ch.sync()
                    ch(sts(rl[:], sm[:, 1:4:2], lamn[:, 0:1], None, ALU.mult, ALU.bypass))
                    ch(sts(am[:, 0:256], ssc[:, 0, 0:256], sm[:, 2:3], None, ALU.mult, ALU.bypass))
                    ch(sts(am[:, 256:384], ssc[:, 0, 256:384], sm[:, 0:1], None, ALU.mult, ALU.bypass))
                    ch.sync()
                    ch(stt(am[:, 0:256], ssc[:, 1, 0:256], rl[:, 1:2], am[:, 0:256], ALU.mult, ALU.add))
                    stt(am[:, 256:384], ssc[:, 1, 256:384], rl[:, 0:1], am[:, 256:384], ALU.mult, ALU.add
                        ).then_inc(s_A, 1)
                    dve.wait_ge(s_E, h + one)
                    for lv in range(LEVELS):
                        dv = lview(XD[:, lv, :], lv)
                        ch(v.tensor_tensor(dv[:, :, 1, :], dv[:, :, 1, :], lview(hq[j], lv)[:, :, 1, :], ALU.mult))
                        ch(v.tensor_tensor(dv[:, :, 0, :], dv[:, :, 0, :], lview(kk[:], lv)[:, :, 0, :], ALU.mult))
                    ch(v.tensor_tensor(XD[:, CROSS, P:T], XD[:, CROSS, P:T], hq[j][:, P:T], ALU.mult))
                    v.tensor_tensor(XD[:, CROSS, 0:P], XD[:, CROSS, 0:P], kk[:, 0:P], ALU.mult).then_inc(s_X, 1)
                    dve.wait_ge(s_zev, h * UNITS + (H0 * UNITS + 6))
                    e = e4[j].rearrange("p t a n -> p (t a n)")
                    ch(sts(e, e, 1.0, None, ALU.add, ALU.bypass))
                    ch.sync()
                    ch(v.reciprocal(e, e))
                    ch.sync()
                    if j == 0:
                        dve.wait_ge(s_pw, g * 32 + (32 * PAIRS * l + 32))
                    ch(v.tensor_tensor(spair[:, :, j, :], e4[j][:, :, 2, :],
                                       psc[:, j:j + 1, :].to_broadcast([P, 2, P]), ALU.mult))
                    ch(v.tensor_tensor(ga[:], e4[j][:, :, 1, :], subg[:].unsqueeze(1).to_broadcast([P, 2, P]), ALU.mult))
                    ch(v.tensor_tensor(gr[:], e4[j][:, :, 0, :], vg[j][:, :, 1, :], ALU.mult))
                    ch.sync()
                    ch(v.tensor_tensor(gr[:], gr[:], e4[j][:, :, 3, :], ALU.mult))
                    ch.sync()
                    ch(v.tensor_tensor(gr[:], gr[:], ng[:].unsqueeze(1).to_broadcast([P, 2, P]), ALU.mult))
                    dve.wait_ge(s_atp, h + one)
                    copy(AT.rearrange("p b q -> p (b q)"), bank(B_S0)[:, 0:384]).then_inc(s_at, 1)
                    dve.wait_ge(s_lv, h + one)
                    ah2 = AH[:, 0:2, :]
                    ch(v.tensor_tensor(ah2, bank(B_O)[:, 0:T].rearrange("p (c t) -> p c t", c=2),
                                       ident[:].unsqueeze(1).to_broadcast([P, 2, P]), ALU.mult))
                    ch(copy(AH[:, 2, :], bank(B_LB)[:, 384:512]))
                    ch.sync()
                    apart(dve)
                    for lv in range(LEVELS):
                        m = 1 << lv
                        b, o = (B_LA, lv * P) if lv < 4 else (B_LB, (lv - 4) * P)
                        i = v.copy_predicated(
                            out=lview(ah2.rearrange("p c t -> p (c t)"), lv)[:, :, 1, :],
                            mask=lmask[:, lv, :].rearrange("p (b m) -> p b m", m=m),
                            data=bank(b)[:, o:o + P].rearrange("p (b m) -> p b m", m=m))
                        if lv < LEVELS - 1:
                            ch(i)
                            ch.sync()
                            apart(dve)
                    i.then_inc(s_AH, 1)
                    dve.wait_ge(s_avp, h + one)
                    ch(copy(osb[:, 0:2, :].rearrange("p a n -> p (a n)"), bank(B_S1)[:, 0:T]))
                    dve.wait_ge(s_op, h + one)
                    ch(copy(osb[:, 2:4, :].rearrange("p a n -> p (a n)"), bank(B_O)[:, 0:T]))
                    ch.sync()
                    for i in range(4):
                        ins = dot(am[:, 0:P], osb[:, i, :], osb[:, i, :], ms[:, i:i + 1])
                        if i < 3:
                            ch(ins)
                            ch.sync()
                    ins.then_inc(s_ms, 1)
                    dve.wait_ge(s_rs, h + (NR * l + 2))
                    for t in range(2):
                        ch(stt(mg[:, t, :], osb[:, t, :], rs[:, t:t + 1], ga[:, t, :], ALU.mult, ALU.mult))
                    for t in range(2):
                        ch(stt(osb[:, 2 + t, :], osb[:, 2 + t, :], rs[:, 2 + t:3 + t], gr[:, t, :], ALU.mult, ALU.mult))
                    ch.sync()
                    i = v.tensor_tensor(mg, mg, osb[:, 2:4, :], ALU.add)
                    if j == 1:
                        ch(i)
                        dve.wait_ge(s_y, g + (PAIRS * l + 1))
                        sp2 = spair[:].rearrange("p t j n -> p t (j n)")
                        ch(v.tensor_tensor(sp2, bank(B_LA).rearrange("p (t n) -> p t n", t=2), sp2, ALU.mult))
                        ch.sync()
                        mp = tok[:, :, bass.ds(g * T, T)]
                        i = v.tensor_tensor(mp, mp, sp2, ALU.add)
                    i.then_inc(s_mix, 1)

                def pair(g):
                    step(g * 2, 0, g, None)
                    step(g * 2 + 1, 1, g, None)

                start = ch.n
                with dve.Fori(0, PAIRS) as g:
                    ch.base, ch.n = g * MIX_CHAIN + start, 0
                    pair(g)
                assert ch.n == MIX_CHAIN, ch.n
                ch.base, ch.n = 0, start + PAIRS * MIX_CHAIN
                evac_hT(3 * l + 1)
                for t in range(NT):
                    dve.wait_ge(s_wod, NT * l + t + 1)
                    for hf in range(2):
                        c0 = hf * 512
                        ch(v.tensor_tensor(tok[:, t, c0:c0 + 512], bank(B_ACC + 2 * t + hf), ada[:, 2, c0:c0 + 512], ALU.mult))
                ch.sync()
                for t in range(NT):
                    ch(v.tensor_tensor(xs[:, t, :], xs[:, t, :], tok[:, t, :], ALU.add))
                ch(copy(g2keep[:], ada[:, 5, :]))
                normed(2 * l + 1, NR * l + HEADS + 1, 3, 4).then_inc(s_tok, 1)
                dve.wait_ge(s_tok, 2 * l + 2)
                copy(cb, cact[:].unsqueeze(2).to_broadcast([P, KC, P])).then_inc(s_dot, 1)
                v.memset(diag[:, 1, GROUP - 1, :], 0.0).then_inc(s_cb, 1)
                evac_hT(3 * l + 2)
                more_ada = l + 1 < DEPTH

                def top8(vals, ids, src):
                    apart(dve)
                    ch(v.max(out=vals, in_=src))
                    ch.sync()
                    apart(dve)
                    ch(v.max_index(ids, vals, src))

                def top16(vals, ids, src, scratch, freed=None):
                    top8(vals[:, 0:8], ids[:, 0:8], src)
                    i = v.match_replace(out=scratch, in_to_replace=vals[:, 0:8], in_values=src, imm_value=-3.4e38)
                    if freed is None:
                        ch(i)
                        ch.sync()
                    else:
                        i.then_inc(s_scfree, 1)
                        dve.wait_ge(s_scfree, freed)
                    top8(vals[:, 8:16], ids[:, 8:16], scratch)

                def route_half(h, t, a):
                    if a == 0:
                        dve.wait_ge(s_psc, h + (HEADS * l + 1))
                    o = (t * 2 + a) * P
                    top16(sv[:, a, :], iu[:, a, :], bank(B_SC)[:, o:o + P], wk,
                          h + (HEADS * l + 1) if t == 1 and a == 1 else None)

                def route_pairs(h, t):
                    ch.sync()
                    cv = cand.rearrange("p (a b) -> p a b", a=TOPK)
                    ch(copy(idf[:], iu[:]))
                    ch(v.tensor_tensor(cv, sv[:, 0, :].unsqueeze(2).to_broadcast([P, TOPK, TOPK]),
                                       sv[:, 1, :].unsqueeze(1).to_broadcast([P, TOPK, TOPK]), ALU.add))
                    ch.sync()
                    top16(ts[:], pos[:], cand, cand2)
                    ch.sync()
                    sts(rmx[:, 0:1], ts[:, 0:1], -1.0, None, ALU.mult, ALU.bypass).then_inc(s_rmx, 1)
                    ch(sts(ab[:, 0, :], pos[:], 4, None, ALU.logical_shift_right, ALU.bypass))
                    ch(sts(ab[:, 1, :], pos[:], 15, None, ALU.bitwise_and, ALU.bypass))
                    ch.sync()
                    ch(copy(abf[:], ab[:]))
                    ch.sync()
                    ch(v.tensor_tensor(oneh, abf[:].unsqueeze(3).to_broadcast([P, 2, TOPK, TOPK]),
                                       iota16[:].unsqueeze(1).unsqueeze(1).to_broadcast([P, 2, TOPK, TOPK]), ALU.is_equal))
                    ch.sync()
                    ch(v.tensor_tensor(oneh, oneh, idf[:].unsqueeze(2).to_broadcast([P, 2, TOPK, TOPK]), ALU.mult))
                    ch.sync()
                    ch(v.tensor_reduce(red[:], oneh, AX, ALU.add))
                    ch.sync()
                    ch(stt(idfl[:], red[:, 0, :], float(P), red[:, 1, :], ALU.mult, ALU.add))
                    ch.sync()

                def route_end(h, t, first=False):
                    if not first:
                        dve.wait_ge(s_vacc, h * HGROUPS + (summed(l) + (t - 1) * GROUPS))
                    sts(idx[t][:], idfl[:], float(NEXP * l), None, ALU.add, ALU.bypass).then_inc(s_route, 1)
                    dve.wait_ge(s_rexp, h * NT + (2 * HEADS * l + t + 1))
                    ch(v.reciprocal(rmx[:, 1:2], rmx[:, 1:2]))
                    ch.sync()
                    ch(sts(gate[t][:], ge[:], rmx[:, 1:2], None, ALU.mult, ALU.bypass))

                def dot_group(h, gi):
                    t = gi // GROUPS
                    dve.wait_ge(s_u[gi % 2], h * (16 * HGROUPS * GROUP // 2) + 64 * (LGROUPS // 2 * l + gi // 2 + 1))
                    for s in range(GROUP):
                        u = ubuf[:, gi % 2, s, :]
                        i = dot(u, u, tok[:, t, :], dots[gi % 2][:, s:s + 1])
                        if s < GROUP - 1:
                            ch(i)
                    i.then_inc(s_dot, 1)

                def diag_group(h, gi):
                    t, q = gi // GROUPS, gi % GROUPS
                    dve.wait_ge(s_gel, h * HGROUPS + (LGROUPS * l + gi + 1))
                    dve.wait_ge(s_vacc, h * HGROUPS + (summed(l) + gi - 1))
                    for s in range(GROUP):
                        k = q * GROUP + s
                        i = sts(diag[:, gi % 2, s, :], ident[:], gel[gi % 2][:, s:s + 1], gate[t][:, k:k + 1],
                                ALU.mult, ALU.mult)
                        if s < GROUP - 1:
                            ch(i)
                    i.then_inc(s_diag, 1)

                r0 = R0

                def head(h, more):
                    for gi in range(HGROUPS):
                        dot_group(h, gi)
                        t, q = gi // GROUPS, gi % GROUPS
                        nh, nt = (h, 1) if t == 0 else (h + 1, 0)
                        if t == 0 or more:
                            if q == 0:
                                route_half(nh, nt, 0)
                            elif q == 1:
                                route_half(nh, nt, 1)
                            elif q == 2:
                                route_pairs(nh, nt)
                                route_end(nh, nt, False)
                        ch.sync()
                        diag_group(h, gi)
                        if more_ada and gi < ADA_PER_HEAD:
                            add_ada(h * 4 + (R0 + 1 + gi), B_ADA[gi % 2], h * (ADA_PER_HEAD * CH) + gi * CH)

                route_half(0, 0, 0)
                route_half(0, 0, 1)
                route_pairs(0, 0)
                route_end(0, 0, True)
                if more_ada:
                    dve.wait_ge(s_bias, 16 * (l + 2))
                start = ch.n
                with dve.Fori(0, HEADS - 1) as h:
                    ch.base, ch.n = h * PEER_CHAIN + start, 0
                    head(h, True)
                assert ch.n == PEER_CHAIN, ch.n
                ch.base, ch.n = 0, start + (HEADS - 1) * PEER_CHAIN
                head(HEADS - 1, False)
                dve.wait_ge(s_vacc, summed(l) + LGROUPS)
                for t in range(NT):
                    for hf in range(2):
                        c0 = hf * 512
                        ch(v.tensor_tensor(tok[:, t, c0:c0 + 512], bank(B_ACC + 2 * t + hf), g2keep[:, c0:c0 + 512], ALU.mult))
                ch.sync()
                ch(v.tensor_tensor(xs[:, 0, :], xs[:, 0, :], tok[:, 0, :], ALU.add))
                v.tensor_tensor(xs[:, 1, :], xs[:, 1, :], tok[:, 1, :], ALU.add).then_inc(s_peer, 1)
                dve.wait_ge(s_peer, l + 1)
            dve.wait_ge(s_gain, 16 * (2 * DEPTH + 1))
            ch(dot(tok[:, 0, :], xs[:, 0, :], xs[:, 0, :], ms[:, 0:1]))
            dot(tok[:, 1, :], xs[:, 1, :], xs[:, 1, :], ms[:, 1:2]).then_inc(s_ms, 1)
            dve.wait_ge(s_rs, NR * DEPTH + 1)
            ch(stt(tok[:, 0, :], xs[:, 0, :], rs[:, 0:1], gain[:], ALU.mult, ALU.mult))
            stt(tok[:, 1, :], xs[:, 1, :], rs[:, 1:2], gain[:], ALU.mult, ALU.mult).then_inc(s_fin, 1)


_INS = ["x", "c", "ada_w", "ada_b", "norm_mix_g", "w_in", "diff_lambda", "diff_subln_g", "pool_w", "pool_scale",
        "hgrn_lower_bounds", "hgrn_norm_g", "w_out", "norm_ffn_g", "peer_w_query", "peer_sub_keys",
        "peer_u", "peer_v", "final_g"]


def kernel(**inputs):
    import numpy as np
    import concourse.bacc as bacc
    from concourse.bass_utils import run_bass_kernel_spmd

    nc = bacc.Bacc("TRN2", target_bir_lowering=False, num_devices=1, dynamic_dma_scratch_size=8192)
    arrays, args = {}, []
    for name in _INS:
        a = np.ascontiguousarray(inputs[name])
        arrays[f"in_{name}"] = a
        args.append(nc.dram_tensor(f"in_{name}", a.shape, mybir.dt.from_np(a.dtype), kind="ExternalInput").ap())
    args.append(nc.dram_tensor("out_0", (1, T, D), F32, kind="ExternalOutput").ap())
    build(nc, *args)
    return run_bass_kernel_spmd(nc, [arrays], core_ids=[0]).results[0]["out_0"]
```

```python
import math
from contextlib import ExitStack

import concourse.bass as bass
from concourse import mybir

F32 = mybir.dt.float32
U32 = mybir.dt.uint32
U8 = mybir.dt.uint8
I32 = mybir.dt.int32
ALU = mybir.AluOpType
ACT = mybir.ActivationFunctionType
AX = mybir.AxisListType.X

P = 128
D = 1024
T = 256
NT = T // P
DEPTH = 2
KC = D // P
HEADS = 8
PAIRS = HEADS // 2
SECT = 11
AQ, AK, AV, PP, HQ, HF, HI, HG, ZA, ZP, ZR = range(SECT)
LEVELS = 7
CROSS = LEVELS
WINDOWS = (2, 4, 8, 16)
EPS = 1e-6
FLOOR = 1e-20
MASKED = -1e33
NEXP = 16384
TOPK = 16
GROUP = 4
GROUPS = TOPK // GROUP
HGROUPS = NT * GROUPS
LGROUPS = HEADS * HGROUPS
CH = 256
ADA_CHUNKS = 2 * D // CH
BLOCKS = (3, 2)
BLOCK0 = (0, 3 * HEADS)
BIG = 2.0 ** 32
LN_BIG = 32 * math.log(2.0)

B_Z = (0, 1, 2)
B_S0, B_S1, B_LA, B_LB, B_O = 3, 4, 5, 6, 7
B_Q, B_SC, B_ADA = 0, 1, (2, 3, 4, 5)
B_ACC = 4
B_WO = ((0, 1), (2, B_LB))
B_KEYS = B_S1
B_H = ((B_S0, B_LA), (B_S1, B_O))
UNITS = 6

MIX_CHAIN = tuple(150 + 2 * n for n in BLOCKS)
PEER_CHAIN = 99


def lambda_init(layer):
    return 0.8 - 0.6 * math.exp(-0.3 * layer)


def mixed(l):
    return (HEADS + 1) * l + 1


def dotted(l):
    return (LGROUPS + 1) * l + 1


def summed(l):
    return (LGROUPS + 4) * l + 4


class Chain:

    def __init__(self, eng, sem):
        self.eng, self.sem, self.base, self.n = eng, sem, 0, 0

    def __call__(self, ins):
        ins.then_inc(self.sem, 1)
        self.n += 1

    def sync(self):
        self.eng.wait_ge(self.sem, self.base + self.n)


def build(nc, x, c, ada_w, ada_b, norm_mix_g, w_in, diff_lambda, diff_subln_g, pool_w, pool_scale,
          hgrn_lower_bounds, hgrn_norm_g, w_out, norm_ffn_g, peer_w_query, peer_sub_keys,
          peer_u, peer_v, final_g, out):
    with ExitStack() as ctx:
        def sb(name, shape, dt=F32):
            return ctx.enter_context(nc.sbuf_tensor(name, shape, dt))

        def sem(name):
            return ctx.enter_context(nc.semaphore(name))

        PS = ctx.enter_context(nc.psum_tensor("PS", [P, 8, 512], F32))

        def bank(b):
            return PS[:, b, :]

        xs = sb("xs", [P, NT, D])
        tok = sb("tok", [P, NT, D])
        hT = sb("hT", [P, KC, T])
        ada = sb("ada", [P, 6, D])
        braw = sb("braw", [P, 2, 4, CH])
        gain = braw[:, 1].rearrange("p k n -> p (k n)")
        ones = sb("ones", [P, P])
        wbuf = [sb(f"wbuf{j}", [P, KC * SECT * P]) for j in range(2)]
        wz = [w[:].rearrange("p (k s n) -> p k s n", k=KC, s=SECT) for w in wbuf]
        wo_sb = wbuf[0][:, 0:KC * D].rearrange("p (k n) -> p k n", k=KC)
        ubuf = wbuf[0][:, 0:2 * GROUP * D].rearrange("p (b s d) -> p b s d", b=2, s=GROUP)
        vbuf = wbuf[1][:, 0:2 * GROUP * D].rearrange("p (b s d) -> p b s d", b=2, s=GROUP)
        ring = [sb(f"ring{j}", [P, KC * CH]) for j in range(2)]
        ringv = [r[:].rearrange("p (k n) -> p k n", k=KC) for r in ring]
        XD = ring[0][:].rearrange("p (l t) -> p l t", l=8)
        PW = 16 + T
        pt = [ring[1][:, i * 2 * PW:(i + 1) * 2 * PW].rearrange("p (h t) -> p h t", h=2) for i in range(2)]
        pooled = ring[1][:, 4 * PW:4 * PW + 2 * T].rearrange("p (h t) -> p h t", h=2)
        AT = ring[1][:, 4 * PW + 2 * T:4 * PW + 2 * T + 384].rearrange("p (b q) -> p b q", b=3)
        MSZ = 3328
        M = sb("M", [P, 2 * MSZ])
        firstv = ringv + [wbuf[1][:, i * KC * CH:(i + 1) * KC * CH].rearrange("p (k n) -> p k n", k=KC)
                          for i in range(2)]

        def mreg(j, off, n):
            return M[:, j * MSZ + off:j * MSZ + off + n]

        qk = [mreg(j, 0, 512).rearrange("p (a t) -> p a t", a=2) for j in range(2)]
        hq = [mreg(j, 512, 256) for j in range(2)]
        e3 = [mreg(j, 768, 768).rearrange("p (a t) -> p a t", a=3) for j in range(2)]
        e4 = [mreg(j, 1536, 1024).rearrange("p (t a n) -> p t a n", t=2, a=4) for j in range(2)]
        vg = [mreg(j, 2560, 512).rearrange("p (t a n) -> p t a n", t=2, a=2) for j in range(2)]
        av = [mreg(j, 3072, 256).rearrange("p (t n) -> p t n", t=2) for j in range(2)]
        cb = M[:, 0:1024].rearrange("p (k n) -> p k n", k=KC)
        diag = M[:, 1024:2048].rearrange("p (b s n) -> p b s n", b=2, s=GROUP)
        qT = M[:, 2048:2560].rearrange("p (a t) -> p a t", a=2)
        keys_raw = M[:, 2560:2816].rearrange("p (a d) -> p a d", a=2)
        keysT = M[:, 2816:3072].rearrange("p (a d) -> p a d", a=2)
        wk = M[:, 3072:3200]
        cand = M[:, 3328:3584]
        cand2 = M[:, 3584:3840]
        oneh = M[:, 3840:4352].rearrange("p (a k n) -> p a k n", a=2, k=TOPK)
        pb = sb("pb", [P, 2, PW])
        pwt = sb("pwt", [P, 2, T])
        psc = sb("psc", [P, 2, P])
        ssc = sb("ssc", [P, 2, 384])
        am = sb("am", [P, 384])
        kk = sb("kk", [P, T])
        bs = sb("bs", [P, T])
        AH = sb("AH", [P, 3, P])
        ga = sb("ga", [P, 2, P])
        gr = sb("gr", [P, 2, P])
        spair = sb("spair", [P, 2, 2, P])
        osb = sb("osb", [P, 4, P])
        ident = sb("ident", [P, P])
        nd = sb("nd", [P, 384])
        lmask = sb("lmask", [P, LEVELS, P], U8)
        resetr = sb("resetr", [P, T])
        rc16 = sb("rc16", [P, 4, 16])
        rw = sb("rw", [P, 4])
        pm = sb("pm", [P, 4, 4])
        slopes = sb("slopes", [P, HEADS])
        iota16 = sb("iota16", [P, 16])
        mhalf = sb("mhalf", [P, 4])
        rows24 = sb("rows24", [24, P])
        col = sb("col", [P, 24])
        cact = sb("cact", [P, 8])
        lbp = sb("lbp", [P, 2, 8])
        lbm = sb("lbm", [P, 2, 8])
        oml = sb("oml", [P, 2, 8])
        dlt = sb("dlt", [P, 2, 8])
        small = sb("small", [P, 48])
        lamr = sb("lamr", [P, 256])
        part = [sb("part", [P, CH])[:], lamr[:]]
        subg = sb("subg", [P, P])
        ng = sb("ng", [P, P])
        lamn = sb("lamn", [P, 1])
        mx = sb("mx", [P, 4])
        sm = sb("sm", [P, 4])
        rl = sb("rl", [P, 2])
        ms = sb("ms", [P, 4])
        rsb = sb("rsb", [P, 4])
        rs = sb("rs", [P, 4])
        sv = sb("sv", [P, 2, TOPK])
        iu = sb("iu", [P, 2, TOPK], U32)
        idf = sb("idf", [P, 2, TOPK])
        ts = sb("ts", [P, TOPK])
        pos = sb("pos", [P, TOPK], U32)
        ab = sb("ab", [P, 2, TOPK], U32)
        abf = sb("abf", [P, 2, TOPK])
        red = sb("red", [P, 2, TOPK])
        idfl = sb("idfl", [P, TOPK])
        idx = [sb(f"idx{t}", [P, TOPK], U32) for t in range(2)]
        ge = sb("ge", [P, TOPK])
        rmx = sb("rmx", [P, 2])
        gate = [sb(f"gate{t}", [P, TOPK]) for t in range(2)]
        dots = [sb(f"dots{b}", [P, GROUP]) for b in range(2)]
        gel = [sb(f"gel{b}", [P, GROUP]) for b in range(2)]

        s_par, s_x, s_bias, s_gain = sem("s_par"), sem("s_x"), sem("s_bias"), sem("s_gain")
        s_small, s_keys, s_wo, s_pw = sem("s_small"), sem("s_keys"), sem("s_wo"), sem("s_pw")
        s_w = [sem("s_w0"), sem("s_w1")]
        s_r = [sem(f"s_r{j}") for j in range(4)]
        s_b = [sem("s_b0"), sem("s_b1")]
        s_bused = sem("s_bused")
        s_part = sem("s_part")
        s_pused = sem("s_pused")
        s_u = [sem("s_u0"), sem("s_u1")]
        s_v = [sem("s_v0"), sem("s_v1")]
        s_out = sem("s_out")
        s_id = sem("s_id")
        s_const = sem("s_const")
        s_cstv = sem("s_cstv")
        s_vc = sem("s_vc")
        s_pc = sem("s_pc")
        s_colps = sem("s_colps")
        s_pcol = sem("s_pcol")
        s_pexp = sem("s_pexp")
        s_cb = sem("s_cb")
        s_chunk = sem("s_chunk")
        s_adaadd = sem("s_adaadd")
        s_gused = sem("s_gused")
        s_lamd, s_lame = sem("s_lamd"), sem("s_lame")
        s_smused = sem("s_smused")
        s_ms, s_rs = sem("s_ms"), sem("s_rs")
        s_tok = sem("s_tok")
        s_tp = sem("s_tp")
        s_hTa, s_hTd = sem("s_hTa"), sem("s_hTd")
        s_z, s_zev = sem("s_z"), sem("s_zev")
        s_F, s_ln = sem("s_F"), sem("s_ln")
        s_sc, s_mx, s_exp = sem("s_sc"), sem("s_mx"), sem("s_exp")
        s_D, s_E, s_X = sem("s_D"), sem("s_E"), sem("s_X")
        s_A, s_atp, s_at, s_avp = sem("s_A"), sem("s_atp"), sem("s_at"), sem("s_avp")
        s_lv, s_AH, s_op = sem("s_lv"), sem("s_AH"), sem("s_op")
        s_pooled, s_y = sem("s_pooled"), sem("s_y")
        s_mix = sem("s_mix")
        s_wod = sem("s_wod")
        s_q0, s_q0ev = sem("s_q0"), sem("s_q0ev")
        s_psc0 = sem("s_psc0")
        s_kt, s_kte = sem("s_kt"), sem("s_kte")
        s_qev, s_psc, s_scfree = sem("s_qev"), sem("s_psc"), sem("s_scfree")
        s_rmx, s_rexp, s_route = sem("s_rmx"), sem("s_rexp"), sem("s_route")
        s_dot, s_gel, s_diag, s_vacc = sem("s_dot"), sem("s_gel"), sem("s_diag"), sem("s_vacc")
        s_peer = sem("s_peer")
        s_fin = sem("s_fin")

        w_in_v = [w_in[l].rearrange("(k p) (s n) -> k p s n", p=P, s=SECT) for l in range(DEPTH)]
        ada_w_v = [ada_w[l].rearrange("(k p) n -> p k n", p=P) for l in range(DEPTH)]
        wq_v = [peer_w_query[l].rearrange("(k p) n -> p k n", p=P) for l in range(DEPTH)]
        u_rows = peer_u.rearrange("l e d -> (l e) d")
        v_rows = peer_v.rearrange("l e d -> (l e) d")

        WTAIL = range(-(-2 * GROUP * D // (SECT * P)), KC)

        def brow(v, n):
            return v.rearrange("(o n) -> o n", o=1).to_broadcast([P, n])

        def block_part(l, jm, p):
            return (jm * BLOCKS[l] + p) % 2

        def block_cols(m, p):
            return m * CH if p == 2 else m * (2 * CH) + (2 * D + p * CH)

        def apart(eng):
            eng.nop(nofuse=True)

        block = ctx.enter_context(nc.Block())

        @block.sync
        def _(sp):
            sp.dma_start(rows24[0:8, :], c.rearrange("o (k n) -> (o k) n", k=8)).then_inc(s_par, 16)
            sp.dma_start(rows24[8:24, :], hgrn_lower_bounds.rearrange("l (k n) -> (l k) n", k=8)
                         ).then_inc(s_par, 16)

            def load_small(l):
                sp.dma_start(lamr[:], brow(diff_lambda[l].rearrange("a n -> (a n)"), 256)).then_inc(s_small, 16)
                sp.dma_start(subg[:], brow(diff_subln_g[l], P)).then_inc(s_small, 16)
                sp.dma_start(ng[:], brow(hgrn_norm_g[l], P)).then_inc(s_small, 16)

            adaf = ada[:].rearrange("p a n -> p (a n)")

            def load_bias_row(l, lo, hi):
                sp.dma_start(adaf[0:1, lo:hi], ada_b[l:l + 1, lo:hi]).then_inc(s_bias, 16)

            def load_gain(v):
                sp.dma_start(gain, brow(v, D)).then_inc(s_gain, 16)

            def load_first(i):
                sp.dma_start(firstv[i % 4], ada_w_v[0][:, :, i * CH:(i + 1) * CH]).then_inc(s_r[i % 4], 16)

            def load_wq(l, h, j):
                sp.dma_start(ringv[j], wq_v[l][:, :, bass.ds(h * CH, CH)]).then_inc(s_r[j], 16)

            for i in range(4):
                load_first(i)
            sp.dma_start(adaf[:, 0:2 * D], brow(ada_b[0, 0:2 * D], 2 * D)).then_inc(s_bias, 16)
            sp.dma_start(xs[:], x[0].rearrange("(t p) d -> p t d", p=P)).then_inc(s_x, 16)
            for i in range(4, ADA_CHUNKS):
                sp.wait_ge(s_chunk, i - 3)
                load_first(i)
                if i == 4:
                    load_gain(norm_mix_g[0])
            load_small(0)

            for l in range(DEPTH):
                def load_w(h, j, chunks=range(KC)):
                    for k in chunks:
                        sp.dma_start(wz[j][:, k], w_in_v[l][k][:, :, bass.ds(h * P, P)]).then_inc(s_w[j], 16)

                def load_pool(g):
                    sp.dma_start(pwt[:], pool_w[l, bass.ds(g, 1), :, :].rearrange("o (h p) d -> p (o h) d", p=P)
                                 ).then_inc(s_pw, 16)
                    sp.dma_start(psc[:].rearrange("p a n -> p (a n)"),
                                 pool_scale[l:l + 1, bass.ds(g * T, T)].to_broadcast([P, T])).then_inc(s_pw, 16)

                def load_blocks(m, first=False):
                    for p in range(BLOCKS[l]):
                        b = m * BLOCKS[l] + (BLOCK0[l] + p)
                        layer = l + 1 if p == 2 else l
                        cols = m * CH if p == 2 else m * (2 * CH) + (2 * D + p * CH)
                        for s in range(2):
                            if not (first and l == 0 and p == 0):
                                sp.wait_ge(s_bused, b * 2 + (s - 1))
                            sp.dma_start(braw[:, s], ada_w_v[layer][:, 4 * s:4 * s + 4, bass.ds(cols, CH)]
                                         ).then_inc(s_b[s], 16)

                if l == 0:
                    load_w(0, 0)
                    sp.wait_ge(s_chunk, ADA_CHUNKS)
                    load_w(1, 1)
                else:
                    load_w(0, 0, WTAIL)
                    load_w(1, 1, WTAIL)
                    sp.wait_ge(s_dot, dotted(l - 1) + LGROUPS)
                    load_w(0, 0, range(WTAIL[0]))
                    sp.wait_ge(s_vacc, summed(l - 1) + LGROUPS)
                    load_w(1, 1, range(WTAIL[0]))
                    sp.wait_ge(s_peer, l)
                    load_bias_row(l, 2 * D, 6 * D)
                load_pool(0)
                sp.wait_ge(s_gused, 2 * l + 1)
                if l == 0:
                    load_bias_row(0, 2 * D, 6 * D)
                    sp.wait_ge(s_tok, 1)
                    load_bias_row(1, 0, 2 * D)
                load_blocks(0, True)
                with sp.Fori(1, PAIRS) as g:
                    for j in range(2):
                        sp.wait_ge(s_z, UNITS * HEADS * l + (g * 2 + (j - 1)) * UNITS)
                        load_w(g * 2 + j, j)
                        load_blocks(g * 2 + (j - 1))
                    sp.wait_ge(s_mix, g * 2 + mixed(l))
                    load_pool(g)
                sp.wait_ge(s_z, UNITS * (HEADS * l + 7))
                sp.dma_start(wo_sb, w_out[l].rearrange("(k p) n -> p k n", p=P)).then_inc(s_wo, 16)
                load_blocks(HEADS - 1)
                sp.wait_ge(s_bused, 2 * (BLOCK0[l] + HEADS * BLOCKS[l]))
                load_gain(norm_ffn_g[l])
                sp.wait_ge(s_mix, mixed(l) + HEADS - 1)
                sp.dma_start(keys_raw, peer_sub_keys[l].rearrange("a k d -> k a d")).then_inc(s_keys, 16)
                sp.wait_ge(s_lv, HEADS * (l + 1))
                load_wq(l, 1, 0)
                sp.wait_ge(s_avp, HEADS * (l + 1))
                sp.wait_ge(s_y, PAIRS * (l + 1))
                load_wq(l, 0, 1)
                sp.wait_ge(s_gused, 2 * l + 2)
                load_gain(norm_mix_g[l + 1] if l + 1 < DEPTH else final_g)
                if l + 1 < DEPTH:
                    load_small(l + 1)
                with sp.Fori(2, HEADS) as h:
                    sp.wait_ge(s_chunk, h + (ADA_CHUNKS + HEADS * l))
                    load_wq(l, h, 0)
            sp.wait_ge(s_fin, 1)
            sp.dma_start(out[0].rearrange("(t p) d -> p t d", p=P), tok[:]).then_inc(s_out, 16)
            sp.wait_ge(s_out, 16)

        @block.gpsimd
        def _(pool):
            pc = Chain(pool, s_pc)
            pc(nc.gpsimd.memset(ident[:], 0.0))
            pc.sync()
            nc.gpsimd.affine_select(out=ident[:], in_=ident[:], compare_op=ALU.not_equal, fill=1.0, base=0,
                                    pattern=[[-1, P]], channel_multiplier=1).then_inc(s_id, 1)
            pc(nc.gpsimd.memset(ones[:], 1.0))
            pc(nc.gpsimd.memset(pb[:], 0.0))
            pc(nc.gpsimd.memset(mhalf[:], -0.5))
            pc(nc.gpsimd.memset(resetr[:], 1.0))
            iscr = hT[:].rearrange("p k t -> p (k t)").bitcast(I32)
            pc(nc.gpsimd.iota(iscr[:, 0:384], pattern=[[1, 384]], base=-P, channel_multiplier=-1))
            pc(nc.gpsimd.iota(iscr[:, 384:400], pattern=[[1, 16]], base=0, channel_multiplier=0))
            fm = tok[:].rearrange("p t d -> p (t d)")[:, 0:LEVELS * P].rearrange("p (l n) -> p l n", l=LEVELS)
            pc(nc.gpsimd.memset(fm, 1.0))
            pc.sync()
            pc(nc.gpsimd.memset(resetr[:, 0:1], 0.0))
            pc(nc.gpsimd.memset(resetr[:, P:P + 1], 0.0))
            for i in range(LEVELS):
                m = 1 << i
                v = fm[:, i, :].rearrange("p (c b m) -> p c b m", c=2, m=m)
                nb = P // 2 // m
                pc.sync()
                pc(nc.gpsimd.affine_select(out=v, in_=v, compare_op=ALU.is_ge, fill=0.0, base=0,
                                           pattern=[[0, 2], [-2 * m, nb], [0, m]], channel_multiplier=1))
                pc.sync()
                last = nc.gpsimd.affine_select(out=v, in_=v, compare_op=ALU.is_ge, fill=0.0, base=m - 1,
                                               pattern=[[0, 2], [2 * m, nb], [0, m]], channel_multiplier=-1)
                if i < LEVELS - 1:
                    pc(last)
            last.then_inc(s_const, 1)
            pool.wait_ge(s_cstv, 1)
            for a in (0, 256):
                n = 256 if a == 0 else 128
                off = 0 if a == 0 else 128
                nc.gpsimd.affine_select(out=nd[:, a:a + n], in_=nd[:, a:a + n], compare_op=ALU.is_ge, fill=MASKED,
                                        base=P - off, pattern=[[-1, n]], channel_multiplier=1).then_inc(s_const, 1)

            def rsqrt(k, n, width, c=0):
                pool.wait_ge(s_ms, k + 1)
                apart(pool)
                pc(nc.gpsimd.tensor_scalar(rsb[:, c:c + n], ms[:, c:c + n], 1.0 / width, EPS, ALU.mult, ALU.add))
                pc.sync()
                nc.gpsimd.tensor_tensor(rs[:, c:c + n], rsb[:, c:c + n], mhalf[:, 0:n], ALU.pow).then_inc(s_rs, 1)

            NR = HEADS + 3
            for l in range(DEPTH):
                rsqrt(NR * l, NT, D)
                pool.wait_ge(s_bias, 16 * (3 + l))
                pool.wait_ge(s_tok, 3 * l + 1)
                tt = nc.gpsimd.tensor_tensor

                def block_sums(m, jm, p, first=False):
                    b = m * BLOCKS[l] + (BLOCK0[l] + p)
                    o = part[block_part(l, jm, p)]
                    for s in range(2):
                        w = braw[:, s]
                        pool.wait_ge(s_b[s], b * 16 + 16)
                        pc(tt(w, w, cact[:, 4 * s:4 * s + 4].unsqueeze(2).to_broadcast([P, 4, CH]), ALU.mult))
                        pc.sync()
                        pc(tt(w[:, 0:2], w[:, 0:2], w[:, 2:4], ALU.add))
                        pc.sync()
                        if s == 0:
                            if not (first and l == 0):
                                pool.wait_ge(s_pused, b - 1)
                            tt(o, w[:, 0], w[:, 1], ALU.add).then_inc(s_bused, 1)
                        else:
                            pc(tt(w[:, 0], w[:, 0], w[:, 1], ALU.add))
                            pc.sync()
                            pool.wait_ge(s_bused, b * 2 + 1)
                            tt(o, o, w[:, 0], ALU.add).then_inc(s_bused, 1)
                    cols = block_cols(m, p)
                    pool.wait_ge(s_bused, b * 2 + 2)
                    tt(o[0:1, :], o[0:1, :], ada[:].rearrange("p a n -> p (a n)")[0:1, bass.ds(cols, CH)], ALU.add
                       ).then_inc(s_part, 1)

                def step(m, jm, more):
                    if BLOCKS[l] == 3:
                        block_sums(m, jm, 2)
                    rsqrt(m + (NR * l + 1), 4, P)
                    if more:
                        block_sums(m + 1, 1 - jm, 0)
                        block_sums(m + 1, 1 - jm, 1)

                block_sums(0, 0, 0, True)
                block_sums(0, 0, 1, True)
                start = pc.n
                with pool.Fori(0, PAIRS - 1) as g:
                    pc.base, pc.n = g * (2 + 10 * BLOCKS[l]) + start, 0
                    step(g * 2, 0, True)
                    step(g * 2 + 1, 1, True)
                assert pc.n == 2 + 10 * BLOCKS[l]
                pc.base, pc.n = 0, start + (PAIRS - 1) * pc.n
                step(HEADS - 2, 0, True)
                step(HEADS - 1, 1, False)
                for t in range(NT):
                    rsqrt(NR * l + HEADS + 1 + t, 1, D, t)

                def gather_u(h, gi):
                    t, q = gi // GROUPS, gi % GROUPS
                    if q == 0:
                        pool.wait_ge(s_route, h * NT + (2 * HEADS * l + t + 1))
                    if l or gi or not isinstance(h, int) or h:
                        pool.wait_ge(s_dot, h * HGROUPS + (dotted(l) + gi - 1))
                    apart(pool)
                    for s in range(GROUP):
                        k = q * GROUP + s
                        nc.gpsimd.indirect_dma_start(
                            out=ubuf[:, gi % 2, s, :], out_offset=None, in_=u_rows,
                            in_offset=bass.IndirectOffsetOnAxis(ap=idx[t][:, k:k + 1], axis=0)).then_inc(s_u[gi % 2], 16)

                def gather_v(h, gi):
                    t, q = gi // GROUPS, gi % GROUPS
                    pool.wait_ge(s_vacc, h * HGROUPS + (summed(l) + gi - 1))
                    apart(pool)
                    for s in range(GROUP):
                        k = q * GROUP + s
                        nc.gpsimd.indirect_dma_start(
                            out=vbuf[:, gi % 2, s, :], out_offset=None, in_=v_rows,
                            in_offset=bass.IndirectOffsetOnAxis(ap=idx[t][:, k:k + 1], axis=0)).then_inc(s_v[gi % 2], 16)

                def head(h, more):
                    for gi in range(HGROUPS):
                        if gi + 1 < HGROUPS:
                            gather_u(h, gi + 1)
                        elif more:
                            gather_u(h + 1, 0)
                        gather_v(h, gi)

                gather_u(0, 0)
                with pool.Fori(0, HEADS - 1) as h:
                    head(h, True)
                head(HEADS - 1, False)
            rsqrt(NR * DEPTH, NT, D)

        @block.scalar
        def _(act):
            act.wait_ge(s_pcol, 1)
            nc.scalar.activation(small[:, 0:8], col[:, 0:8], ACT.Exp, scale=-1.0)
            nc.scalar.activation(lbp[:].rearrange("p a n -> p (a n)"), small[:, 8:24], ACT.Exp).then_inc(s_pexp, 1)

            def evac_hT(l, n, b):
                act.wait_ge(s_tp, 12 * l + 4 * n + b + 1)
                nc.scalar.activation(hT[:, 2 * b:2 * b + 2, :].rearrange("p k t -> p (k t)"), bank(b),
                                     ACT.Copy).then_inc(s_hTa, 1)

            for l in range(DEPTH):
                act.wait_ge(s_lamd, l + 1)
                nc.scalar.activation(small[:, 26:28], small[:, 24:26], ACT.Exp).then_inc(s_lame, 1)
                for b in range(2):
                    evac_hT(l, 0, b)
                H0 = HEADS * l

                def unit_ready(n, u):
                    act.wait_ge(s_z, (n + H0) * UNITS + (u + 1))

                def evac(n, j, u, g=None):
                    b = bank(B_Z[u % 3])
                    unit_ready(n, u)
                    if u == 0:
                        nc.scalar.mul(qk[j][:, 0, :], b[:, 0:T], 0.125)
                        nc.scalar.activation(qk[j][:, 1, :], b[:, T:2 * T], ACT.Copy).then_inc(s_zev, 1)
                    elif u == 1:
                        nc.scalar.activation(hq[j], b[:, 0:T], ACT.Copy)
                        nc.scalar.activation(e3[j][:, 0:2, :].rearrange("p a t -> p (a t)"), b, ACT.Exp, scale=-1.0)
                        nc.scalar.activation(e3[j][:, 2, :], b[:, T:2 * T], ACT.Exp).then_inc(s_zev, 1)
                    elif u == 2:
                        nc.scalar.activation(pb[:, j, 16:16 + T], b[:, 0:T], ACT.Copy).then_inc(s_zev, 1)
                    elif u in (3, 4):
                        nc.scalar.activation(vg[j][:, u - 3].rearrange("p a n -> p (a n)"), b[:, 0:256], ACT.Copy)
                        nc.scalar.activation(e4[j][:, u - 3, 0:3].rearrange("p a n -> p (a n)"), b[:, 128:512],
                                             ACT.Exp, scale=-1.0).then_inc(s_zev, 1)
                    else:
                        bv = b.rearrange("p (t a n) -> p t a n", t=2, a=2)
                        nc.scalar.activation(av[j], bv[:, :, 0, :], ACT.Copy)
                        nc.scalar.activation(e4[j][:, :, 3, :], bv[:, :, 1, :], ACT.Exp, scale=-1.0).then_inc(s_zev, 1)

                def step(n, m, jm, g):
                    jn = 1 - jm
                    act.wait_ge(s_F, m + (H0 + 1))
                    nc.scalar.activation(XD[:, 3, :], XD[:, 0, :], ACT.Ln).then_inc(s_ln, 1)
                    if n is not None:
                        if not (isinstance(n, int) and n < 2 and l == 0):
                            act.wait_ge(s_mix, n + (mixed(l) - 1))
                        evac(n, jn, 0)
                    else:
                        for b in range(3):
                            evac_hT(l, 1, b)
                    act.wait_ge(s_mx, m + (H0 + 1))
                    for t in range(2):
                        for a in range(2):
                            cols = slice(256, 384) if t == 0 else slice(0, 256)
                            i = nc.scalar.activation(ssc[:, a, cols], ssc[:, a, cols], ACT.Exp,
                                                     bias=mx[:, 2 * t + a:2 * t + a + 1],
                                                     accum_out=sm[:, 2 * t + a:2 * t + a + 1])
                    i.then_inc(s_exp, 1)
                    act.wait_ge(s_D, m + (H0 + 1))
                    xf = XD.rearrange("p l t -> p (l t)")
                    nc.scalar.activation(xf, xf, ACT.Exp).then_inc(s_E, 1)
                    if n is not None:
                        evac(n, jn, 1)
                        if jn == 0:
                            act.wait_ge(s_pooled, g + (PAIRS * l + 1))
                        evac(n, jn, 2)
                        for u in range(3, UNITS):
                            evac(n, jn, u)

                if l:
                    act.wait_ge(s_mix, mixed(l) - 1)
                for u in range(UNITS):
                    evac(0, 0, u)
                with act.Fori(0, PAIRS - 1) as g:
                    step(g * 2 + 1, g * 2, 0, g)
                    step(g * 2 + 2, g * 2 + 1, 1, g)
                step(HEADS - 1, HEADS - 2, 0, PAIRS - 1)
                step(None, HEADS - 1, 1, PAIRS - 1)
                act.wait_ge(s_kt, l + 1)
                nc.scalar.activation(keysT.rearrange("p a d -> p (a d)"), bank(B_KEYS)[:, 0:256],
                                     ACT.Copy).then_inc(s_kte, 1)
                evac_hT(l, 1, 3)

                for t in range(NT):
                    for i in range(2):
                        act.wait_ge(s_tp, 12 * l + 8 + 2 * t + i + 1)
                        nc.scalar.activation(hT[:, 4 * i:4 * i + 4, t * P:(t + 1) * P],
                                             bank(B_H[t][i]).rearrange("p (k n) -> p k n", k=4), ACT.Copy
                                             ).then_inc(s_hTa, 1)
                    if t == 0:
                        act.wait_ge(s_q0, l + 1)
                    else:
                        act.wait_ge(s_chunk, ADA_CHUNKS + HEADS * l + 1)
                    nc.scalar.activation(qT[:, :, t * P:(t + 1) * P],
                                         bank(2 * t)[:, 0:2 * P].rearrange("p (a n) -> p a n", a=2), ACT.Copy
                                         ).then_inc(s_q0ev if t == 0 else s_qev, 1)
                def q_evac(h):
                    act.wait_ge(s_chunk, h + (ADA_CHUNKS + HEADS * l + 1))
                    nc.scalar.activation(qT.rearrange("p a t -> p (a t)"), bank(B_Q), ACT.Copy).then_inc(s_qev, 1)

                def route_exp(h, t):
                    act.wait_ge(s_rmx, h * NT + (2 * HEADS * l + t + 1))
                    nc.scalar.activation(ge[:], ts[:], ACT.Exp, bias=rmx[:, 0:1],
                                         accum_out=rmx[:, 1:2]).then_inc(s_rexp, 1)

                def head(h, more):
                    for gi in range(HGROUPS):
                        act.wait_ge(s_dot, h * HGROUPS + (dotted(l) + gi + 1))
                        nc.scalar.activation(gel[gi % 2][:], dots[gi % 2][:], ACT.Gelu).then_inc(s_gel, 1)
                        if gi == 2:
                            route_exp(h, 1)
                            if more:
                                q_evac(h + 1)
                        if gi == GROUPS + 2 and more:
                            route_exp(h + 1, 0)

                route_exp(0, 0)
                with act.Fori(0, HEADS - 1) as h:
                    head(h, True)
                head(HEADS - 1, False)

        @block.tensor
        def _(pe):
            mm = nc.tensor.matmul

            pe.wait_ge(s_id, 1)
            pe.wait_ge(s_par, 32)
            nc.tensor.transpose(bank(B_Q)[:, 0:24], rows24[:], ident[0:24, 0:24]).then_inc(s_colps, 1)

            pe.wait_ge(s_cb, 1)
            for n in range(ADA_CHUNKS):
                pe.wait_ge(s_r[n % 4], 16 * (n // 4 + 1))
                if n >= 4:
                    pe.wait_ge(s_adaadd, n - 3)
                for k in range(KC):
                    i = mm(bank(B_ADA[n % 4])[:, 0:CH], cb[:, k, :], firstv[n % 4][:, k, :],
                           start=(k == 0), stop=(k == KC - 1))
                i.then_inc(s_chunk, 1)

            def transpose_tok(b):
                for k in (2 * b, 2 * b + 1):
                    for t in range(NT):
                        o = (k % 2) * T + t * P
                        i = nc.tensor.transpose(bank(b)[:, o:o + P], tok[:, t, k * P:(k + 1) * P], ident[:])
                i.then_inc(s_tp, 1)

            NR = HEADS + 3
            for l in range(DEPTH):
                H0 = HEADS * l
                pe.wait_ge(s_tok, 3 * l + 1)
                for b in range(4):
                    transpose_tok(b)
                pe.wait_ge(s_hTa, 10 * l + 2)
                pe.wait_ge(s_hTd, 2 * l + 2)

                def project(n, j, u):
                    b = bank(B_Z[u % 3])
                    if u == 0:
                        pe.wait_ge(s_w[j], (n - j) * (64) + (64 * H0 + 128))
                    if not (isinstance(n, int) and n == 0 and u < 3):
                        pe.wait_ge(s_zev, (n + H0) * UNITS + (u - 2))
                    elif l:
                        pe.wait_ge(s_zev, H0 * UNITS)
                    if u < 3:
                        for i, s in enumerate(((AQ, AK), (HQ, HF), (PP,))[u]):
                            for k in range(KC):
                                ins = mm(b[:, i * T:(i + 1) * T], wz[j][:, k, s, :], hT[:, k, :],
                                         start=(k == 0), stop=(k == KC - 1))
                    elif u in (3, 4):
                        t = u - 3
                        for k in range(KC):
                            ins = mm(b, hT[:, k, t * P:(t + 1) * P], wz[j][:, k, HI:ZP + 1, :],
                                     start=(k == 0), stop=(k == KC - 1))
                    else:
                        for t in range(NT):
                            for k in range(KC):
                                ins = mm(b[:, t * 256:(t + 1) * 256], hT[:, k, t * P:(t + 1) * P],
                                         wz[j][:, k, AV:ZR + 1:ZR - AV, :], start=(k == 0), stop=(k == KC - 1))
                    ins.then_inc(s_z, 1)

                def out_proj(t, hf, chunks):
                    for k in chunks:
                        i = mm(bank(B_WO[t][hf]), hT[:, k, t * P:(t + 1) * P], wo_sb[:, k, hf * 512:(hf + 1) * 512],
                               start=(k == 0), stop=(k == KC - 1))
                    return i

                def step(n, m, jm, g):
                    jn = 1 - jm
                    one = H0 + 1

                    def block_total(p, dst):
                        pe.wait_ge(s_part, m * BLOCKS[l] + (BLOCK0[l] + p + 1))
                        mm(dst, ones[:], part[block_part(l, jm, p)], start=True, stop=True).then_inc(s_pused, 1)

                    def proj(u):
                        if n is not None:
                            project(n, jn, u)
                        elif u == 0:
                            pe.wait_ge(s_zev, UNITS * (H0 + HEADS))
                            pe.wait_ge(s_mix, mixed(l) + HEADS - 2)
                            for b in range(3):
                                transpose_tok(b)
                        elif u == 1:
                            pe.wait_ge(s_hTa, 10 * l + 5)
                            pe.wait_ge(s_wo, 16 * (l + 1))
                            out_proj(0, 0, range(KC - 2))
                            out_proj(0, 1, range(KC - 2))
                        elif u == 3:
                            out_proj(1, 0, range(KC - 2))

                    proj(0)
                    pe.wait_ge(s_ms, m + (NR * l + 1))
                    pe.wait_ge(s_zev, (m + H0) * UNITS + 1)
                    for a, b in enumerate((B_S0, B_S1)):
                        r = slice(64 * a, 64 * a + 64)
                        mm(bank(b)[:, 0:256], qk[jm][r, 0, P:T], qk[jm][r, 1, :], start=True, stop=True)
                        i = mm(bank(b)[:, 256:384], qk[jm][r, 0, 0:P], qk[jm][r, 1, 0:P], start=True, stop=True)
                    i.then_inc(s_sc, 1)
                    proj(1)
                    proj(2)
                    proj(3)
                    pe.wait_ge(s_X, m + one)
                    for lv in range(LEVELS + 1):
                        if lv == CROSS:
                            i = mm(bank(B_LB)[:, 384:512], XD[:, lv, 0:P], XD[:, lv, P:T], start=True, stop=True)
                            continue
                        b, o = (B_LA, lv * P) if lv < 4 else (B_LB, (lv - 4) * P)
                        for ck in range(2):
                            right = XD[:, lv, ck * P:(ck + 1) * P].rearrange(
                                "p (b w m) -> p b w m", w=2, m=1 << lv)[:, :, 1, :]
                            mm(bank(b)[:, o + 64 * ck:o + 64 * ck + 64], XD[:, lv, ck * P:(ck + 1) * P], right,
                               start=True, stop=True)
                    for ck in range(2):
                        i = mm(bank(B_O)[:, ck * P:(ck + 1) * P], kk[:, ck * P:(ck + 1) * P],
                               hq[jm][:, ck * P:(ck + 1) * P], start=True, stop=True)
                    i.then_inc(s_lv, 1)
                    block_total(0, bank(B_S1)[:, 256:512])
                    pe.wait_ge(s_A, m + one)
                    for b in range(3):
                        i = nc.tensor.transpose(bank(B_S0)[:, b * P:(b + 1) * P], am[:, b * P:(b + 1) * P], ident[:])
                    i.then_inc(s_atp, 1)
                    proj(4)
                    pe.wait_ge(s_at, m + one)
                    mm(bank(B_S1)[:, 0:P], AT[:, 2, :], av[jm][:, 0, :], start=True, stop=True)
                    mm(bank(B_S1)[:, P:2 * P], AT[:, 0, :], av[jm][:, 0, :], start=True, stop=False)
                    mm(bank(B_S1)[:, P:2 * P], AT[:, 1, :], av[jm][:, 1, :], start=False, stop=True
                       ).then_inc(s_avp, 1)
                    pe.wait_ge(s_AH, m + one)
                    block_total(1, bank(B_O)[:, 256:512])
                    if BLOCKS[l] == 3:
                        block_total(2, bank(B_LB)[:, 0:256])
                    mm(bank(B_O)[:, 0:P], AH[:, 0, :], vg[jm][:, 0, 0, :], start=True, stop=True)
                    mm(bank(B_O)[:, P:2 * P], AH[:, 1, :], vg[jm][:, 1, 0, :], start=True, stop=False)
                    mm(bank(B_O)[:, P:2 * P], AH[:, 2, :], vg[jm][:, 0, 0, :], start=False, stop=True
                       ).then_inc(s_op, 1)
                    if jm == 1:
                        pe.wait_ge(s_pooled, g + (PAIRS * l + 1))
                        pe.wait_ge(s_pw, g * 32 + (32 * PAIRS * l + 32))
                        for t in range(NT):
                            for hf in range(2):
                                i = mm(bank(B_LA)[:, t * T:(t + 1) * T], pooled[:, hf, t * P:(t + 1) * P],
                                       pwt[:, hf, :], start=(hf == 0), stop=(hf == 1))
                        i.then_inc(s_y, 1)
                    proj(5)

                for u in range(UNITS):
                    project(0, 0, u)
                with pe.Fori(0, PAIRS - 1) as g:
                    step(g * 2 + 1, g * 2, 0, g)
                    step(g * 2 + 2, g * 2 + 1, 1, g)
                step(HEADS - 1, HEADS - 2, 0, PAIRS - 1)
                step(None, HEADS - 1, 1, PAIRS - 1)

                pe.wait_ge(s_ms, NR * l + HEADS + 1)
                pe.wait_ge(s_keys, 16 * (l + 1))
                for a in range(2):
                    i = nc.tensor.transpose(bank(B_KEYS)[:, a * P:(a + 1) * P], keys_raw[:, a, :], ident[:])
                i.then_inc(s_kt, 1)
                out_proj(1, 1, range(KC - 2))
                pe.wait_ge(s_mix, mixed(l) + HEADS)
                transpose_tok(3)
                pe.wait_ge(s_hTa, 10 * l + 6)
                for t in range(NT):
                    for hf in range(2):
                        i = out_proj(t, hf, (KC - 2, KC - 1))
                    i.then_inc(s_wod, 1)

                for t in range(NT):
                    pe.wait_ge(s_tok, 3 * l + 2 + t)
                    if t == 1:
                        pe.wait_ge(s_kte, l + 1)
                    for k in range(KC):
                        i = nc.tensor.transpose(bank(B_H[t][k // 4])[:, k % 4 * P:(k % 4 + 1) * P],
                                                tok[:, t, k * P:(k + 1) * P], ident[:])
                        if k % 4 == 3:
                            i.then_inc(s_tp, 1)
                    pe.wait_ge(s_hTa, 10 * l + 8 + 2 * t)
                    if t == 0:
                        pe.wait_ge(s_r[1], 16 * (ADA_CHUNKS // 4 + l + 1))
                    for a in range(2):
                        for k in range(KC):
                            i = mm(bank(2 * t)[:, a * P:(a + 1) * P], ringv[1][:, k, a * P:(a + 1) * P],
                                   hT[:, k, t * P:(t + 1) * P], start=(k == 0), stop=(k == KC - 1))
                    i.then_inc(s_q0 if t == 0 else s_chunk, 1)
                    if t == 0:
                        pe.wait_ge(s_q0ev, l + 1)
                        pe.wait_ge(s_kte, l + 1)
                        for a in range(2):
                            i = mm(bank(B_SC)[:, a * P:(a + 1) * P], qT[:, a, 0:P], keysT[:, a, :], start=True, stop=True)
                        i.then_inc(s_psc0, 1)

                def queries(h):
                    pe.wait_ge(s_r[0], h * 16 + 16 * (ADA_CHUNKS // 4 + (HEADS - 1) * l))
                    for a in range(2):
                        for k in range(KC):
                            i = mm(bank(B_Q)[:, a * T:(a + 1) * T], ringv[0][:, k, a * P:(a + 1) * P], hT[:, k, :],
                                   start=(k == 0), stop=(k == KC - 1))
                    i.then_inc(s_chunk, 1)

                def key_scores(h):
                    pe.wait_ge(s_qev, h + (HEADS * l + 1))
                    pe.wait_ge(s_scfree, h + HEADS * l)
                    for t in range(NT):
                        for a in range(2):
                            o = (t * 2 + a) * P
                            i = mm(bank(B_SC)[:, o:o + P], qT[:, a, t * P:(t + 1) * P], keysT[:, a, :],
                                   start=True, stop=True)
                    i.then_inc(s_psc, 1)

                def expert_sum(h, gi, last=False):
                    t = gi // GROUPS
                    pe.wait_ge(s_diag, h * HGROUPS + (LGROUPS * l + gi + 1))
                    pe.wait_ge(s_v[gi % 2], h * (16 * HGROUPS * GROUP // 2)
                               + 64 * (LGROUPS // 2 * l + gi // 2 + 1))
                    for s in range(GROUP):
                        for hf in range(2):
                            i = mm(bank(B_ACC + 2 * t + hf), diag[:, gi % 2, s, :],
                                   vbuf[:, gi % 2, s, hf * 512:(hf + 1) * 512], start=False,
                                   stop=(last and s == GROUP - 1), skip_group_check=True)
                    i.then_inc(s_vacc, 1)

                def head(h, more):
                    for gi in range(HGROUPS):
                        if more and gi == 3:
                            key_scores(h + 1)
                        expert_sum(h, gi, not more and gi % GROUPS == GROUPS - 1)
                        if more and gi == 2:
                            queries(h + 1)

                pe.wait_ge(s_cb, l + 2)
                for b in range(4):
                    i = mm(bank(B_ACC + b), diag[:, 1, GROUP - 1, :], hT[:, 0:2, :], start=True, stop=False,
                           skip_group_check=True)
                    i.then_inc(s_vacc, 1)
                pe.wait_ge(s_qev, HEADS * l + 1)
                pe.wait_ge(s_rmx, 2 * HEADS * l + 1)
                for a in range(2):
                    i = mm(bank(B_SC)[:, (2 + a) * P:(3 + a) * P], qT[:, a, P:T], keysT[:, a, :], start=True, stop=True)
                i.then_inc(s_psc, 1)
                with pe.Fori(0, HEADS - 1) as h:
                    head(h, True)
                head(HEADS - 1, False)

        @block.vector
        def _(dve):
            v = nc.vector
            ch = Chain(dve, s_vc)

            def copy(o, i):
                return v.tensor_copy(o, i)

            def sts(o, a, s1, s2, op0, op1):
                return v.tensor_scalar(o, a, s1, s2, op0, op1)

            def stt(o, a, s, b, op0, op1):
                return v.scalar_tensor_tensor(out=o, in0=a, scalar=s, in1=b, op0=op0, op1=op1)

            def dot(o, a, b, acc):
                return v.tensor_tensor_reduce(out=o, in0=a, in1=b, scale=1.0, scalar=0.0, op0=ALU.mult,
                                              op1=ALU.add, accum_out=acc)

            def mean_squares(tiles):
                for t in tiles:
                    i = dot(tok[:, t, :], xs[:, t, :], xs[:, t, :], ms[:, t:t + 1])
                    if t != tiles[-1]:
                        ch(i)
                i.then_inc(s_ms, 1)

            for h in range(HEADS):
                ch(v.memset(slopes[:, h:h + 1], 2.0 ** -(h + 1)))
            ch(v.memset(pm[:], 0.0))
            ch.sync()
            for g in range(4):
                ch(v.memset(pm[:, g, 0:g + 1], 1.0))
                ch(v.memset(rw[:, g:g + 1], 1.0 / WINDOWS[g]))
            dve.wait_ge(s_colps, 1)
            ch(copy(col[:], bank(B_Q)[:, 0:24]))
            ch.sync()
            ch(v.tensor_tensor(small[:, 32:40], col[:, 8:16], col[:, 16:24], ALU.max))
            ch.sync()
            ch(v.tensor_tensor(small[:, 8:16], col[:, 8:16], small[:, 32:40], ALU.subtract))
            v.tensor_tensor(small[:, 16:24], col[:, 16:24], small[:, 32:40], ALU.subtract).then_inc(s_pcol, 1)
            dve.wait_ge(s_pexp, 1)
            ch(sts(small[:, 0:8], small[:, 0:8], 1.0, None, ALU.add, ALU.bypass))
            ch(v.tensor_tensor(small[:, 32:40], lbp[:, 0, :], lbp[:, 1, :], ALU.add))
            ch.sync()
            ch(v.reciprocal(small[:, 0:8], small[:, 0:8]))
            ch(v.reciprocal(small[:, 32:40], small[:, 32:40]))
            ch.sync()
            ch(v.tensor_tensor(cact[:], col[:, 0:8], small[:, 0:8], ALU.mult))
            ch(v.tensor_tensor(lbp[:], lbp[:], small[:, 32:40].unsqueeze(1).to_broadcast([P, 2, 8]), ALU.mult))
            ch.sync()
            copy(cb, cact[:].unsqueeze(2).to_broadcast([P, KC, P])).then_inc(s_cb, 1)
            ch(v.tensor_tensor(lbp[:, 1, :], lbp[:, 0, :], lbp[:, 1, :], ALU.add))
            ch.sync()
            ch(v.tensor_tensor(lbp[:, 1, :], lbp[:, 1, :], lbp[:, 0, :], ALU.subtract))
            ch.sync()
            ch(v.memset(lbp[:, 0, :], 0.0))
            ch.sync()
            ch(sts(lbm[:], lbp[:], FLOOR, None, ALU.max, ALU.bypass))
            ch(sts(oml[:], lbp[:], -1.0, 1.0, ALU.mult, ALU.add))
            ch.sync()
            ch(v.tensor_tensor(dlt[:], lbm[:], lbp[:], ALU.subtract))

            dve.wait_ge(s_id, 1)
            dve.wait_ge(s_const, 1)
            iscr = hT[:].rearrange("p k t -> p (k t)").bitcast(I32)
            fm = tok[:].rearrange("p t d -> p (t d)")[:, 0:LEVELS * P].rearrange("p (l n) -> p l n", l=LEVELS)
            ch(copy(lmask[:], fm))
            ch(copy(iota16[:], iscr[:, 384:400]))
            ch(copy(nd[:, 256:384], iscr[:, 128:256]))
            copy(nd[:, 0:256], iscr[:, 0:256]).then_inc(s_cstv, 1)
            ch.sync()
            for g in range(4):
                ch(sts(rc16[:, g, :], iota16[:], 1.0, float(WINDOWS[g]), ALU.add, ALU.min))
            ch.sync()
            ch(v.reciprocal(rc16[:], rc16[:]))
            def add_ada(r, b, col0):
                dve.wait_ge(s_chunk, r + 1)
                a = ada[:].rearrange("p a n -> p (a n)")[:, bass.ds(col0, CH)]
                v.tensor_tensor(a, bank(b)[:, 0:CH], a, ALU.add).then_inc(s_adaadd, 1)

            dve.wait_ge(s_bias, 16)
            for i in range(ADA_CHUNKS):
                add_ada(i, B_ADA[i % 4], i * CH)
                if i == 3:
                    dve.wait_ge(s_x, 16)
                    ch.sync()
                    mean_squares((0, 1))

            def fold_gain(n, sc):
                dve.wait_ge(s_gain, 16 * (n + 1))
                ch.sync()
                stt(ada[:, sc, :], ada[:, sc, :], 1.0, gain, ALU.add, ALU.mult).then_inc(s_gused, 1)

            def normed(n, k, sh, sc, tiles):
                dve.wait_ge(s_rs, k + 1)
                dve.wait_ge(s_gused, n + 1)
                for t in tiles:
                    ch(stt(tok[:, t, :], xs[:, t, :], rs[:, t:t + 1], ada[:, sc, :], ALU.mult, ALU.mult))
                ch.sync()
                for t in tiles:
                    i = v.tensor_tensor(tok[:, t, :], tok[:, t, :], ada[:, sh, :], ALU.add)
                    if t != tiles[-1]:
                        ch(i)
                i.then_inc(s_tok, 1)

            def evac_hT(l):
                for b in (2, 3):
                    dve.wait_ge(s_tp, 12 * l + b + 1)
                    copy(hT[:, 2 * b:2 * b + 2, :].rearrange("p k t -> p (k t)"), bank(b)).then_inc(s_hTd, 1)

            NR = HEADS + 3
            dve.wait_ge(s_const, 3)
            dve.wait_ge(s_adaadd, ADA_CHUNKS)
            for l in range(DEPTH):
                H0 = HEADS * l
                dve.wait_ge(s_small, 48 * (l + 1))
                ch(dot(lamr[:, 0:64], lamr[:, 0:64], lamr[:, 64:128], small[:, 24:25]))
                dot(lamr[:, 128:192], lamr[:, 128:192], lamr[:, 192:256], small[:, 25:26]).then_inc(s_lamd, 1)
                dve.wait_ge(s_lame, l + 1)
                ch(stt(lamn[:], small[:, 27:28], -lambda_init(l), small[:, 26:27], ALU.add, ALU.subtract))
                sts(subg[:], subg[:], 1.0 - lambda_init(l), None, ALU.mult, ALU.bypass).then_inc(s_mix, 1)
                fold_gain(2 * l, 1)
                if l:
                    mean_squares((1,))
                normed(2 * l, NR * l, 0, 1, (0, 1))
                evac_hT(l)

                def lview(a, lv):
                    return a.rearrange("p (b w m) -> p b w m", w=2, m=1 << lv)

                def block_out(h, p, src):
                    ch(copy(ada[:].rearrange("p a n -> p (a n)")[:, bass.ds(block_cols(h, p), CH)], src))

                def forget(h, j):
                    dve.wait_ge(s_zev, h * UNITS + (H0 * UNITS + 2))
                    e = e3[j].rearrange("p a t -> p (a t)")
                    ch(sts(e, e, 1.0, None, ALU.add, ALU.bypass))
                    ch.sync()
                    ch(v.reciprocal(e, e))
                    ch.sync()
                    ch(sts(XD[:, 2, :], e3[j][:, 1, :], oml[:, l, bass.ds(h, 1)], lbm[:, l, bass.ds(h, 1)], ALU.mult, ALU.add))
                    ch(sts(kk[:], e3[j][:, 2, :], oml[:, l, bass.ds(h, 1)], dlt[:, l, bass.ds(h, 1)], ALU.mult, ALU.subtract))
                    ch(v.tensor_tensor(hq[j], hq[j], e3[j][:, 0, :], ALU.mult))
                    ch.sync()
                    ch(sts(XD[:, 1, :], XD[:, 2, :], 1.0 / BIG, BIG, ALU.is_lt, ALU.mult))
                    ch.sync()
                    stt(XD[:, 0, :], XD[:, 1, :], 1.0, XD[:, 2, :], ALU.add, ALU.mult).then_inc(s_F, 1)

                def gates(h, j, g):
                    dve.wait_ge(s_zev, h * UNITS + (H0 * UNITS + 6))
                    e = e4[j].rearrange("p t a n -> p (t a n)")
                    ch(sts(e, e, 1.0, None, ALU.add, ALU.bypass))
                    ch.sync()
                    ch(v.reciprocal(e, e))
                    ch.sync()
                    if j == 0:
                        dve.wait_ge(s_pw, g * 32 + (32 * PAIRS * l + 32))
                    ch(v.tensor_tensor(spair[:, :, j, :], e4[j][:, :, 2, :],
                                       psc[:, j:j + 1, :].to_broadcast([P, 2, P]), ALU.mult))
                    ch(v.tensor_tensor(ga[:], e4[j][:, :, 1, :], subg[:].unsqueeze(1).to_broadcast([P, 2, P]), ALU.mult))
                    ch(v.tensor_tensor(gr[:], e4[j][:, :, 0, :], vg[j][:, :, 1, :], ALU.mult))
                    ch.sync()
                    ch(v.tensor_tensor(gr[:], gr[:], e4[j][:, :, 3, :], ALU.mult))
                    ch.sync()
                    ch(v.tensor_tensor(gr[:], gr[:], ng[:].unsqueeze(1).to_broadcast([P, 2, P]), ALU.mult))

                def step(h, j, g, more=True):
                    one = H0 + 1
                    mg = tok[:, :, bass.ds(h * P, P)]
                    if j == 1:
                        dve.wait_ge(s_zev, h * UNITS + (H0 * UNITS + 3))
                        src = pb[:]
                        for k in range(4):
                            d, lo = 1 << k, (2 << k) - 1
                            dst = pt[k % 2]
                            ch(stt(dst[:, :, lo:PW], src[:, :, lo - d:PW - d], pm[:, bass.ds(g, 1), k:k + 1].rearrange("p a b -> p (a b)"),
                                   src[:, :, lo:PW], ALU.mult, ALU.add))
                            ch.sync()
                            src = dst
                        p0 = pb[:, :, 16:32]
                        ch(stt(pooled[:, :, 16:T], src[:, :, 32:PW], rw[:, bass.ds(g, 1)], pb[:, :, 32:PW],
                               ALU.mult, ALU.subtract))
                        ch(v.tensor_tensor(pooled[:, :, 0:16], src[:, :, 16:32],
                                           rc16[:, bass.ds(g, 1), :].to_broadcast([P, 2, 16]), ALU.mult))
                        ch.sync()
                        v.tensor_tensor(pooled[:, :, 0:16], pooled[:, :, 0:16], p0, ALU.subtract).then_inc(s_pooled, 1)
                    dve.wait_ge(s_sc, h + one)
                    for a, b in enumerate((B_S0, B_S1)):
                        ch(stt(ssc[:, a, :], nd[:], slopes[:, bass.ds(h, 1)], bank(b)[:, 0:384], ALU.mult, ALU.add))
                    ch.sync()
                    ch(v.tensor_reduce(mx[:, 0:2], ssc[:, :, 256:384], AX, ALU.max))
                    ch(v.tensor_reduce(mx[:, 2:4], ssc[:, :, 0:256], AX, ALU.max))
                    ch.sync()
                    sts(mx[:], mx[:], -1.0, None, ALU.mult, ALU.bypass).then_inc(s_mx, 1)
                    dve.wait_ge(s_ln, h + one)
                    ch(stt(XD[:, 3, :], XD[:, 1, :], -LN_BIG / BIG, XD[:, 3, :], ALU.mult, ALU.add))
                    ch.sync()
                    ch(v.tensor_tensor_scan(bs[:], resetr[:], XD[:, 3, :], 0.0, ALU.mult, ALU.add))
                    ch.sync()
                    for lv in range(LEVELS):
                        m = 1 << lv
                        dv, bv = lview(XD[:, lv, :], lv), lview(bs[:], lv)
                        mid = bv[:, :, 0, m - 1:m].to_broadcast([P, P // m, m])
                        ch(v.tensor_tensor(dv[:, :, 1, :], bv[:, :, 1, :], mid, ALU.subtract))
                        ch(v.tensor_tensor(dv[:, :, 0, :], mid, bv[:, :, 0, :], ALU.subtract))
                    ch(copy(XD[:, CROSS, P:T], bs[:, P:T]))
                    v.tensor_tensor(XD[:, CROSS, 0:P], bs[:, P - 1:P].to_broadcast([P, P]), bs[:, 0:P],
                                    ALU.subtract).then_inc(s_D, 1)
                    dve.wait_ge(s_exp, h + one)
                    ch(v.reciprocal(sm[:], sm[:]))
                    ch.sync()
                    ch(sts(rl[:], sm[:, 1:4:2], lamn[:, 0:1], None, ALU.mult, ALU.bypass))
                    ch(sts(am[:, 0:256], ssc[:, 0, 0:256], sm[:, 2:3], None, ALU.mult, ALU.bypass))
                    ch(sts(am[:, 256:384], ssc[:, 0, 256:384], sm[:, 0:1], None, ALU.mult, ALU.bypass))
                    ch.sync()
                    ch(stt(am[:, 0:256], ssc[:, 1, 0:256], rl[:, 1:2], am[:, 0:256], ALU.mult, ALU.add))
                    stt(am[:, 256:384], ssc[:, 1, 256:384], rl[:, 0:1], am[:, 256:384], ALU.mult, ALU.add
                        ).then_inc(s_A, 1)
                    dve.wait_ge(s_E, h + one)
                    for lv in range(LEVELS):
                        dv = lview(XD[:, lv, :], lv)
                        ch(v.tensor_tensor(dv[:, :, 1, :], dv[:, :, 1, :], lview(hq[j], lv)[:, :, 1, :], ALU.mult))
                        ch(v.tensor_tensor(dv[:, :, 0, :], dv[:, :, 0, :], lview(kk[:], lv)[:, :, 0, :], ALU.mult))
                    ch(v.tensor_tensor(XD[:, CROSS, P:T], XD[:, CROSS, P:T], hq[j][:, P:T], ALU.mult))
                    v.tensor_tensor(XD[:, CROSS, 0:P], XD[:, CROSS, 0:P], kk[:, 0:P], ALU.mult).then_inc(s_X, 1)
                    gates(h, j, g)
                    dve.wait_ge(s_atp, h + one)
                    copy(AT.rearrange("p b q -> p (b q)"), bank(B_S0)[:, 0:384]).then_inc(s_at, 1)
                    dve.wait_ge(s_lv, h + one)
                    ah2 = AH[:, 0:2, :]
                    ch(v.tensor_tensor(ah2, bank(B_O)[:, 0:T].rearrange("p (c t) -> p c t", c=2),
                                       ident[:].unsqueeze(1).to_broadcast([P, 2, P]), ALU.mult))
                    ch(copy(AH[:, 2, :], bank(B_LB)[:, 384:512]))
                    ch.sync()
                    apart(dve)
                    for lv in range(LEVELS):
                        m = 1 << lv
                        b, o = (B_LA, lv * P) if lv < 4 else (B_LB, (lv - 4) * P)
                        i = v.copy_predicated(
                            out=lview(ah2.rearrange("p c t -> p (c t)"), lv)[:, :, 1, :],
                            mask=lmask[:, lv, :].rearrange("p (b m) -> p b m", m=m),
                            data=bank(b)[:, o:o + P].rearrange("p (b m) -> p b m", m=m))
                        if lv < LEVELS - 1:
                            ch(i)
                            ch.sync()
                            apart(dve)
                    i.then_inc(s_AH, 1)
                    dve.wait_ge(s_avp, h + one)
                    ch(copy(osb[:, 0:2, :].rearrange("p a n -> p (a n)"), bank(B_S1)[:, 0:T]))
                    block_out(h, 0, bank(B_S1)[:, 256:512])
                    if more:
                        forget(h + 1, 1 - j)
                    dve.wait_ge(s_op, h + one)
                    ch(copy(osb[:, 2:4, :].rearrange("p a n -> p (a n)"), bank(B_O)[:, 0:T]))
                    block_out(h, 1, bank(B_O)[:, 256:512])
                    if BLOCKS[l] == 3:
                        block_out(h, 2, bank(B_LB)[:, 0:256])
                    ch.sync()
                    for i in range(4):
                        ins = dot(am[:, 0:P], osb[:, i, :], osb[:, i, :], ms[:, i:i + 1])
                        if i < 3:
                            ch(ins)
                            ch.sync()
                    ins.then_inc(s_ms, 1)
                    dve.wait_ge(s_rs, h + (NR * l + 2))
                    for t in range(2):
                        ch(stt(mg[:, t, :], osb[:, t, :], rs[:, t:t + 1], ga[:, t, :], ALU.mult, ALU.mult))
                    for t in range(2):
                        ch(stt(osb[:, 2 + t, :], osb[:, 2 + t, :], rs[:, 2 + t:3 + t], gr[:, t, :], ALU.mult, ALU.mult))
                    ch.sync()
                    i = v.tensor_tensor(mg, mg, osb[:, 2:4, :], ALU.add)
                    if j == 1:
                        ch(i)
                        dve.wait_ge(s_y, g + (PAIRS * l + 1))
                        sp2 = spair[:].rearrange("p t j n -> p t (j n)")
                        ch(v.tensor_tensor(sp2, bank(B_LA).rearrange("p (t n) -> p t n", t=2), sp2, ALU.mult))
                        ch.sync()
                        mp = tok[:, :, bass.ds(g * T, T)]
                        i = v.tensor_tensor(mp, mp, sp2, ALU.add)
                    i.then_inc(s_mix, 1)

                forget(0, 0)
                start = ch.n
                with dve.Fori(0, PAIRS - 1) as g:
                    ch.base, ch.n = g * MIX_CHAIN[l] + start, 0
                    step(g * 2, 0, g)
                    step(g * 2 + 1, 1, g)
                assert ch.n == MIX_CHAIN[l], ch.n
                ch.base, ch.n = 0, start + (PAIRS - 1) * MIX_CHAIN[l]
                step(HEADS - 2, 0, PAIRS - 1)
                step(HEADS - 1, 1, PAIRS - 1, False)
                fold_gain(2 * l + 1, 4)
                for t in range(NT):
                    dve.wait_ge(s_wod, NT * l + t + 1)
                    for hf in range(2):
                        c0 = hf * 512
                        ch(v.tensor_tensor(tok[:, t, c0:c0 + 512], bank(B_WO[t][hf]), ada[:, 2, c0:c0 + 512], ALU.mult))
                    ch.sync()
                    ch(v.tensor_tensor(xs[:, t, :], xs[:, t, :], tok[:, t, :], ALU.add))
                    ch.sync()
                    mean_squares((t,))
                    normed(2 * l + 1, NR * l + HEADS + 1 + t, 3, 4, (t,))
                dve.wait_ge(s_tok, 3 * l + 3)
                v.memset(dots[1][:], 0.0).then_inc(s_dot, 1)
                v.memset(diag[:, 1, GROUP - 1, :], 0.0).then_inc(s_cb, 1)

                def top8(vals, ids, src):
                    apart(dve)
                    ch(v.max(out=vals, in_=src))
                    ch.sync()
                    apart(dve)
                    ch(v.max_index(ids, vals, src))

                def top16(vals, ids, src, scratch, freed=None):
                    top8(vals[:, 0:8], ids[:, 0:8], src)
                    i = v.match_replace(out=scratch, in_to_replace=vals[:, 0:8], in_values=src, imm_value=-3.4e38)
                    if freed is None:
                        ch(i)
                        ch.sync()
                    else:
                        i.then_inc(s_scfree, 1)
                        dve.wait_ge(s_scfree, freed)
                    top8(vals[:, 8:16], ids[:, 8:16], scratch)

                def route_half(h, t, a, first=False):
                    if first:
                        dve.wait_ge(s_psc0, l + 1)
                    elif a == 0:
                        dve.wait_ge(s_psc, h + (HEADS * l + 1))
                    o = (t * 2 + a) * P
                    top16(sv[:, a, :], iu[:, a, :], bank(B_SC)[:, o:o + P], wk,
                          h + (HEADS * l + 1) if t == 1 and a == 1 else None)

                def route_pairs(h, t):
                    ch.sync()
                    cv = cand.rearrange("p (a b) -> p a b", a=TOPK)
                    ch(copy(idf[:], iu[:]))
                    ch(v.tensor_tensor(cv, sv[:, 0, :].unsqueeze(2).to_broadcast([P, TOPK, TOPK]),
                                       sv[:, 1, :].unsqueeze(1).to_broadcast([P, TOPK, TOPK]), ALU.add))
                    ch.sync()
                    top16(ts[:], pos[:], cand, cand2)
                    ch.sync()
                    sts(rmx[:, 0:1], ts[:, 0:1], -1.0, None, ALU.mult, ALU.bypass).then_inc(s_rmx, 1)
                    ch(sts(ab[:, 0, :], pos[:], 4, None, ALU.logical_shift_right, ALU.bypass))
                    ch(sts(ab[:, 1, :], pos[:], 15, None, ALU.bitwise_and, ALU.bypass))
                    ch.sync()
                    ch(copy(abf[:], ab[:]))
                    ch.sync()
                    ch(v.tensor_tensor(oneh, abf[:].unsqueeze(3).to_broadcast([P, 2, TOPK, TOPK]),
                                       iota16[:].unsqueeze(1).unsqueeze(1).to_broadcast([P, 2, TOPK, TOPK]), ALU.is_equal))
                    ch.sync()
                    ch(v.tensor_tensor(oneh, oneh, idf[:].unsqueeze(2).to_broadcast([P, 2, TOPK, TOPK]), ALU.mult))
                    ch.sync()
                    ch(v.tensor_reduce(red[:], oneh, AX, ALU.add))
                    ch.sync()
                    ch(stt(idfl[:], red[:, 0, :], float(P), red[:, 1, :], ALU.mult, ALU.add))
                    ch.sync()

                def route_end(h, t, first=False):
                    if not first:
                        dve.wait_ge(s_vacc, h * HGROUPS + (summed(l) + (t - 1) * GROUPS))
                    sts(idx[t][:], idfl[:], float(NEXP * l), None, ALU.add, ALU.bypass).then_inc(s_route, 1)
                    dve.wait_ge(s_rexp, h * NT + (2 * HEADS * l + t + 1))
                    ch(v.reciprocal(rmx[:, 1:2], rmx[:, 1:2]))
                    ch.sync()
                    ch(sts(gate[t][:], ge[:], rmx[:, 1:2], None, ALU.mult, ALU.bypass))

                def dot_group(h, gi):
                    t = gi // GROUPS
                    dve.wait_ge(s_u[gi % 2], h * (16 * HGROUPS * GROUP // 2) + 64 * (LGROUPS // 2 * l + gi // 2 + 1))
                    for s in range(GROUP):
                        u = ubuf[:, gi % 2, s, :]
                        i = dot(u, u, tok[:, t, :], dots[gi % 2][:, s:s + 1])
                        if s < GROUP - 1:
                            ch(i)
                    i.then_inc(s_dot, 1)

                def diag_group(h, gi):
                    t, q = gi // GROUPS, gi % GROUPS
                    dve.wait_ge(s_gel, h * HGROUPS + (LGROUPS * l + gi + 1))
                    dve.wait_ge(s_vacc, h * HGROUPS + (summed(l) + gi - 1))
                    for s in range(GROUP):
                        k = q * GROUP + s
                        i = sts(diag[:, gi % 2, s, :], ident[:], gel[gi % 2][:, s:s + 1], gate[t][:, k:k + 1],
                                ALU.mult, ALU.mult)
                        if s < GROUP - 1:
                            ch(i)
                    i.then_inc(s_diag, 1)

                def add_experts(t):
                    dve.wait_ge(s_vacc, summed(l) + LGROUPS - (NT - 1 - t) * GROUPS)
                    for hf in range(2):
                        c0 = hf * 512
                        ch(v.tensor_tensor(tok[:, t, c0:c0 + 512], bank(B_ACC + 2 * t + hf), ada[:, 5, c0:c0 + 512], ALU.mult))
                    ch.sync()
                    return v.tensor_tensor(xs[:, t, :], xs[:, t, :], tok[:, t, :], ALU.add)

                def head(h, more):
                    for gi in range(HGROUPS):
                        if gi == HGROUPS - 2 and not more:
                            ch(add_experts(0))
                            ch.sync()
                            ch(dot(tok[:, 0, :], xs[:, 0, :], xs[:, 0, :], ms[:, 0:1]))
                        dot_group(h, gi)
                        t, q = gi // GROUPS, gi % GROUPS
                        nh, nt = (h, 1) if t == 0 else (h + 1, 0)
                        if t == 0 or more:
                            if q == 0:
                                route_half(nh, nt, 0)
                            elif q == 1:
                                route_half(nh, nt, 1)
                            elif q == 2:
                                route_pairs(nh, nt)
                                route_end(nh, nt, False)
                        ch.sync()
                        diag_group(h, gi)

                route_half(0, 0, 0, True)
                route_half(0, 0, 1, True)
                route_pairs(0, 0)
                route_end(0, 0, True)
                start = ch.n
                with dve.Fori(0, HEADS - 1) as h:
                    ch.base, ch.n = h * PEER_CHAIN + start, 0
                    head(h, True)
                assert ch.n == PEER_CHAIN, ch.n
                ch.base, ch.n = 0, start + (HEADS - 1) * PEER_CHAIN
                head(HEADS - 1, False)
                add_experts(1).then_inc(s_peer, 1)
                dve.wait_ge(s_peer, l + 1)
            dve.wait_ge(s_gain, 16 * (2 * DEPTH + 1))
            ch.sync()
            mean_squares((1,))
            dve.wait_ge(s_rs, NR * DEPTH + 1)
            ch(stt(tok[:, 0, :], xs[:, 0, :], rs[:, 0:1], gain, ALU.mult, ALU.mult))
            stt(tok[:, 1, :], xs[:, 1, :], rs[:, 1:2], gain, ALU.mult, ALU.mult).then_inc(s_fin, 1)


_INS = ["x", "c", "ada_w", "ada_b", "norm_mix_g", "w_in", "diff_lambda", "diff_subln_g", "pool_w", "pool_scale",
        "hgrn_lower_bounds", "hgrn_norm_g", "w_out", "norm_ffn_g", "peer_w_query", "peer_sub_keys",
        "peer_u", "peer_v", "final_g"]


def kernel(**inputs):
    import numpy as np
    import concourse.bacc as bacc
    from concourse.bass_utils import run_bass_kernel_spmd

    nc = bacc.Bacc("TRN2", target_bir_lowering=False, num_devices=1, dynamic_dma_scratch_size=8192)
    arrays, args = {}, []
    for name in _INS:
        a = np.ascontiguousarray(inputs[name])
        arrays[f"in_{name}"] = a
        args.append(nc.dram_tensor(f"in_{name}", a.shape, mybir.dt.from_np(a.dtype), kind="ExternalInput").ap())
    args.append(nc.dram_tensor("out_0", (1, T, D), F32, kind="ExternalOutput").ap())
    build(nc, *args)
    return run_bass_kernel_spmd(nc, [arrays], core_ids=[0]).results[0]["out_0"]
```
